# Optimizing a Trainium2 kernel written in Bass

```python
import math
import jax, jax.numpy as jnp
from jax import lax
import numpy as np

D_MODEL = 2048
BATCH = 1
SEQ = 256
DEPTH = 2

N_EVEN = (DEPTH + 1) // 2
N_ODD = DEPTH // 2
D_FF = 4 * D_MODEL
MIX_WIDTH = D_MODEL
EPS = 1e-6
NEG = -1e30

GLA_HEADS = 4
GLA_WIDTH = MIX_WIDTH // 2
GLA_DV = GLA_WIDTH // GLA_HEADS
GLA_DK = GLA_DV // 2
GLA_RANK = 16
GLA_GATE_TAU = 16.0
GLA_CHUNK = 64

NSA_HEADS = 16
NSA_GROUPS = 4
NSA_HPG = NSA_HEADS // NSA_GROUPS
NSA_DH = (MIX_WIDTH - GLA_WIDTH) // NSA_HEADS
CMP_LEN = 32
CMP_STRIDE = 16
SEL_BLOCK = 64
N_SELECT = 16
WINDOW = 512
Q_BLOCK = 128
SEL_Q_CHUNK = 16

ML_HEADS = 4
ML_DV = MIX_WIDTH // ML_HEADS
ML_DQK = ML_DV // 2
ML_CONV = 4
ML_CHUNK = 64

GLA_COLS = 2 * GLA_HEADS * GLA_DK + 2 * GLA_WIDTH + GLA_RANK
NSA_COLS = NSA_HEADS * NSA_DH + 6 * NSA_GROUPS * NSA_DH + 3 * NSA_HEADS
AB_COLS = GLA_COLS + NSA_COLS
ML_COLS = 2 * ML_HEADS * ML_DQK + 2 * MIX_WIDTH + 2 * ML_HEADS

kernel_name = "hybrid_gla_nsa_mlstm_adaln"

def split_last(t, sizes):
    cuts = [int(s) for s in np.cumsum(sizes)[:-1]]
    return jnp.split(t, cuts, axis=-1)

def rmsnorm(x, g):
    xf = x.astype(jnp.float32)
    y = xf * lax.rsqrt(jnp.mean(xf * xf, axis=-1, keepdims=True) + EPS)
    return (y * g.astype(jnp.float32)).astype(x.dtype)

def ada_mod(c, w, b):
    m = jnp.einsum('bd,de->be', jax.nn.silu(c), w) + b
    shift, scale, gate = jnp.split(m[:, None, :], 3, axis=-1)
    return shift, scale, gate

def gla_chunked(q, k, v, log_a):
    B, S, H, DK = q.shape
    DV = v.shape[-1]
    L = GLA_CHUNK
    N = S // L

    def chunks(t):
        return t.reshape(B, N, L, H, t.shape[-1]).transpose(1, 0, 3, 2, 4)

    qc, kc, vc, ac = chunks(q * DK ** -0.5), chunks(k), chunks(v), chunks(log_a)
    causal = jnp.tril(jnp.ones((L, L), bool))

    def step(state, inp):
        qq, kk, vv, aa = inp
        cum = jnp.cumsum(aa.astype(jnp.float32), axis=2)
        q_dec = qq * jnp.exp(cum)
        k_dec = kk * jnp.exp(-cum)
        att = jnp.where(causal, jnp.einsum('bhtd,bhsd->bhts', q_dec, k_dec), 0.0)
        o = jnp.einsum('bhts,bhsv->bhtv', att, vv) + jnp.einsum('bhtd,bhdv->bhtv', q_dec, state)
        total = cum[:, :, -1:, :]
        k_end = kk * jnp.exp(total - cum)
        state = state * jnp.exp(total[:, :, 0, :, None]) + jnp.einsum('bhsd,bhsv->bhdv', k_end, vv)
        return state, o

    state0 = jnp.zeros((B, H, DK, DV), jnp.float32)
    _, o = lax.scan(step, state0, (qc, kc, vc, ac))
    return o.transpose(1, 0, 3, 2, 4).reshape(B, S, H, DV)

def gla_branch(p, w_gate, b_gate, norm_g):
    B, S, _ = p.shape
    q, k, v, r, z = split_last(p, [GLA_HEADS * GLA_DK, GLA_HEADS * GLA_DK, GLA_WIDTH, GLA_WIDTH, GLA_RANK])
    log_a = jax.nn.log_sigmoid((z @ w_gate + b_gate).astype(jnp.float32)) / GLA_GATE_TAU
    heads = lambda t, d: t.reshape(B, S, GLA_HEADS, d)
    o = gla_chunked(heads(q, GLA_DK), heads(k, GLA_DK), heads(v, GLA_DV), heads(log_a, GLA_DK))
    o = rmsnorm(o, norm_g) * jax.nn.silu(heads(r, GLA_DV))
    return o.reshape(B, S, GLA_WIDTH).astype(p.dtype)

def compress_tokens(t, pos, w1, w2):
    B, S, G, Dh = t.shape
    sub = t.reshape(B, S // CMP_STRIDE, CMP_STRIDE, G, Dh)
    blk = jnp.concatenate([sub[:, :-1], sub[:, 1:]], axis=2)
    blk = blk + pos[None, None, :, None, :]
    nc = blk.shape[1]
    flat = blk.transpose(0, 1, 3, 2, 4).reshape(B, nc, G, CMP_LEN * Dh)
    hid = jax.nn.silu(jnp.einsum('bngf,fe->bnge', flat, w1))
    return jnp.einsum('bnge,ed->bngd', hid, w2)

def compressed_attention(q, k_cmp, v_cmp):
    S = q.shape[1]
    nc = k_cmp.shape[1]
    logits = jnp.einsum('btghd,bngd->bghtn', q, k_cmp).astype(jnp.float32) * NSA_DH ** -0.5
    t = jnp.arange(S)
    blk_end = jnp.arange(nc) * CMP_STRIDE + CMP_LEN - 1
    valid = blk_end[None, :] <= t[:, None]
    p = jax.nn.softmax(jnp.where(valid, logits, NEG), axis=-1) * valid
    o = jnp.einsum('bghtn,bngd->btghd', p.astype(v_cmp.dtype), v_cmp)
    return o, p

def select_blocks(p_cmp, S):
    ns = S // SEL_BLOCK
    nc = p_cmp.shape[-1]
    c_start = jnp.arange(nc) * CMP_STRIDE
    s_start = jnp.arange(ns) * SEL_BLOCK
    overlap = ((c_start[:, None] <= s_start[None, :] + SEL_BLOCK - 1)
               & (c_start[:, None] + CMP_LEN - 1 >= s_start[None, :])).astype(jnp.float32)
    imp = jnp.einsum('bghtn,nj->bgtj', p_cmp, overlap)
    cur = jnp.arange(S) // SEL_BLOCK
    j = jnp.arange(ns)
    causal = j[None, :] <= cur[:, None]
    forced = (j[None, :] == 0) | (j[None, :] == cur[:, None]) | (j[None, :] == cur[:, None] - 1)
    imp = jnp.where(forced, jnp.inf, jnp.where(causal, imp, -jnp.inf))
    _, idx = lax.top_k(imp, min(N_SELECT, ns))
    return idx

def selected_attention(q, k, v, idx):
    B, S, G, HPG, Dh = q.shape
    ns = S // SEL_BLOCK
    n_sel = idx.shape[-1]
    kb = k.reshape(B, ns, SEL_BLOCK, G, Dh).transpose(0, 3, 1, 2, 4)
    vb = v.reshape(B, ns, SEL_BLOCK, G, Dh).transpose(0, 3, 1, 2, 4)
    nq = S // SEL_Q_CHUNK
    q_ch = q.reshape(B, nq, SEL_Q_CHUNK, G, HPG, Dh).transpose(1, 0, 2, 3, 4, 5)
    idx_ch = idx.reshape(B, G, nq, SEL_Q_CHUNK, n_sel).transpose(2, 0, 1, 3, 4)
    pos_ch = jnp.arange(S).reshape(nq, SEL_Q_CHUNK)
    bi = jnp.arange(B)[:, None, None, None]
    gi = jnp.arange(G)[None, :, None, None]
    offs = jnp.arange(SEL_BLOCK)

    def one_chunk(args):
        qq, ii, tt = args
        kk = kb[bi, gi, ii]
        vv = vb[bi, gi, ii]
        logits = jnp.einsum('bqghd,bgqnkd->bghqnk', qq, kk).astype(jnp.float32) * Dh ** -0.5
        key_pos = ii[..., None] * SEL_BLOCK + offs
        ok = key_pos <= tt[None, None, :, None, None]
        logits = jnp.where(ok[:, :, None], logits, NEG)
        shp = logits.shape
        p = jax.nn.softmax(logits.reshape(shp[:-2] + (-1,)), axis=-1).reshape(shp)
        return jnp.einsum('bghqnk,bgqnkd->bqghd', p.astype(vv.dtype), vv)

    o = lax.map(one_chunk, (q_ch, idx_ch, pos_ch))
    return o.transpose(1, 0, 2, 3, 4, 5).reshape(B, S, G, HPG, Dh)

def window_attention(q, k, v):
    B, S, G, HPG, Dh = q.shape
    kp = jnp.pad(k, ((0, 0), (WINDOW, 0), (0, 0), (0, 0)))
    vp = jnp.pad(v, ((0, 0), (WINDOW, 0), (0, 0), (0, 0)))
    nqb = S // Q_BLOCK
    q_bl = q.reshape(B, nqb, Q_BLOCK, G, HPG, Dh).transpose(1, 0, 2, 3, 4, 5)
    span = WINDOW + Q_BLOCK

    def one_block(args):
        qq, i = args
        start = i * Q_BLOCK
        kk = lax.dynamic_slice_in_dim(kp, start, span, axis=1)
        vv = lax.dynamic_slice_in_dim(vp, start, span, axis=1)
        tq = start + jnp.arange(Q_BLOCK)
        sk = start - WINDOW + jnp.arange(span)
        diff = tq[:, None] - sk[None, :]
        ok = (diff >= 0) & (diff < WINDOW) & (sk[None, :] >= 0)
        logits = jnp.einsum('bqghd,bkgd->bghqk', qq, kk).astype(jnp.float32) * Dh ** -0.5
        p = jax.nn.softmax(jnp.where(ok, logits, NEG), axis=-1)
        return jnp.einsum('bghqk,bkgd->bqghd', p.astype(vv.dtype), vv)

    o = lax.map(one_block, (q_bl, jnp.arange(nqb)))
    return o.transpose(1, 0, 2, 3, 4, 5).reshape(B, S, G, HPG, Dh)

def nsa_branch(p, q_g, k_g, pos_k, pos_v, ck_w1, ck_w2, cv_w1, cv_w2):
    B, S, _ = p.shape
    G, HPG, Dh = NSA_GROUPS, NSA_HPG, NSA_DH
    kv = G * Dh
    q, kc, vc, ks, vs, kw, vw, gt = split_last(p, [NSA_HEADS * Dh, kv, kv, kv, kv, kv, kv, 3 * NSA_HEADS])
    grp = lambda t: t.reshape(B, S, G, Dh)
    q = rmsnorm(q.reshape(B, S, G, HPG, Dh), q_g)
    k_cmp = rmsnorm(compress_tokens(grp(kc), pos_k, ck_w1, ck_w2), k_g)
    v_cmp = compress_tokens(grp(vc), pos_v, cv_w1, cv_w2)
    k_slc, v_slc = rmsnorm(grp(ks), k_g), grp(vs)
    k_win, v_win = rmsnorm(grp(kw), k_g), grp(vw)
    o_cmp, p_cmp = compressed_attention(q, k_cmp, v_cmp)
    idx = select_blocks(p_cmp, S)
    o_slc = selected_attention(q, k_slc, v_slc, idx)
    o_win = window_attention(q, k_win, v_win)
    g = jax.nn.sigmoid(gt.astype(jnp.float32)).reshape(B, S, G, HPG, 3)
    o = g[..., 0:1] * o_cmp + g[..., 1:2] * o_slc + g[..., 2:3] * o_win
    return o.reshape(B, S, NSA_HEADS * Dh).astype(p.dtype)

def gla_nsa_mixer(h, w_in, w_out, gla_w_gate, gla_b_gate, gla_norm_g, nsa_q_g, nsa_k_g,
                  pos_k, pos_v, ck_w1, ck_w2, cv_w1, cv_w2):
    proj = h @ w_in
    p_gla, p_nsa = split_last(proj, [GLA_COLS, NSA_COLS])
    o_gla = gla_branch(p_gla, gla_w_gate, gla_b_gate, gla_norm_g)
    o_nsa = nsa_branch(p_nsa, nsa_q_g, nsa_k_g, pos_k, pos_v, ck_w1, ck_w2, cv_w1, cv_w2)
    return jnp.concatenate([o_gla, o_nsa], axis=-1) @ w_out

def causal_conv(x, w):
    K = w.shape[0]
    S = x.shape[1]
    xp = jnp.pad(x, ((0, 0), (K - 1, 0), (0, 0)))
    y = xp[:, 0:S] * w[0]
    for j in range(1, K):
        y = y + xp[:, j:j + S] * w[j]
    return y

def mlstm_chunked(q, k, v, log_i, log_f):
    B, S, H, DK = q.shape
    DV = v.shape[-1]
    L = ML_CHUNK
    N = S // L

    def chunks(t):
        return t.reshape(B, N, L, H, t.shape[-1]).transpose(1, 0, 3, 2, 4)

    qc, kc, vc = chunks(q * DK ** -0.5), chunks(k), chunks(v)
    ic = chunks(log_i[..., None])[..., 0]
    fc = chunks(log_f[..., None])[..., 0]
    causal = jnp.tril(jnp.ones((L, L), bool))

    def step(carry, inp):
        C, n, m = carry
        qq, kk, vv, li, lf = inp
        li = li.astype(jnp.float32)
        b = jnp.cumsum(lf.astype(jnp.float32), axis=-1)
        log_d = jnp.where(causal, b[..., :, None] - b[..., None, :] + li[..., None, :], -jnp.inf)
        log_inter = b + m[..., None]
        m_comb = jnp.maximum(log_inter, jnp.max(log_d, axis=-1))
        d = jnp.exp(log_d - m_comb[..., None])
        w_inter = jnp.exp(log_inter - m_comb)
        s = jnp.einsum('bhtd,bhsd->bhts', qq, kk) * d
        num = jnp.einsum('bhts,bhsv->bhtv', s, vv) + w_inter[..., None] * jnp.einsum('bhtd,bhdv->bhtv', qq, C)
        den = jnp.sum(s, axis=-1) + w_inter * jnp.einsum('bhtd,bhd->bht', qq, n)
        h = num / jnp.maximum(jnp.abs(den), jnp.exp(-m_comb))[..., None]
        total = b[..., -1]
        log_w = total[..., None] - b + li
        m_new = jnp.maximum(total + m, jnp.max(log_w, axis=-1))
        w = jnp.exp(log_w - m_new[..., None])
        decay = jnp.exp(total + m - m_new)
        C = decay[..., None, None] * C + jnp.einsum('bhs,bhsd,bhsv->bhdv', w, kk, vv)
        n = decay[..., None] * n + jnp.einsum('bhs,bhsd->bhd', w, kk)
        return (C, n, m_new), h

    carry0 = (jnp.zeros((B, H, DK, DV), jnp.float32), jnp.zeros((B, H, DK), jnp.float32),
              jnp.zeros((B, H), jnp.float32))
    _, h = lax.scan(step, carry0, (qc, kc, vc, ic, fc))
    return h.transpose(1, 0, 3, 2, 4).reshape(B, S, H, DV)

def mlstm_mixer(h, w_in, w_out, conv_w, b_i, b_f, norm_g):
    B, S, _ = h.shape
    proj = h @ w_in
    qk, v, og, gi, gf = split_last(proj, [2 * ML_HEADS * ML_DQK, MIX_WIDTH, MIX_WIDTH, ML_HEADS, ML_HEADS])
    qk = jax.nn.silu(causal_conv(qk, conv_w))
    q, k = jnp.split(qk, 2, axis=-1)
    log_i = (gi + b_i).astype(jnp.float32)
    log_f = jax.nn.log_sigmoid((gf + b_f).astype(jnp.float32))
    hh = mlstm_chunked(q.reshape(B, S, ML_HEADS, ML_DQK), k.reshape(B, S, ML_HEADS, ML_DQK),
                       v.reshape(B, S, ML_HEADS, ML_DV), log_i, log_f)
    hh = rmsnorm(hh, norm_g) * jax.nn.sigmoid(og.reshape(B, S, ML_HEADS, ML_DV))
    return hh.reshape(B, S, MIX_WIDTH).astype(h.dtype) @ w_out

def sqrelu_mlp(h, w1, w2):
    return jnp.square(jax.nn.relu(h @ w1)) @ w2

def setup_inputs(seed: int = 0) -> dict:
    key = jax.random.key(seed)
    ks = iter(jax.random.split(key, 40))

    def nrm(shape, scale):
        return jax.random.normal(next(ks), shape, jnp.float32) * scale

    def gain(shape):
        return 1.0 + nrm(shape, 0.1)

    D = D_MODEL
    return {
        "x": nrm((BATCH, SEQ, D), 1.0),
        "c": nrm((BATCH, D), 1.0),
        "norm_mix_g": gain((DEPTH, D)),
        "mod_mix_w": nrm((DEPTH, D, 3 * D), 0.5 * D ** -0.5),
        "mod_mix_b": nrm((DEPTH, 3 * D), 0.02),
        "norm_mlp_g": gain((DEPTH, D)),
        "mod_mlp_w": nrm((DEPTH, D, 3 * D), 0.5 * D ** -0.5),
        "mod_mlp_b": nrm((DEPTH, 3 * D), 0.02),
        "mlp_w1": nrm((DEPTH, D, D_FF), D ** -0.5),
        "mlp_w2": nrm((DEPTH, D_FF, D), D_FF ** -0.5),
        "ab_w_in": nrm((N_EVEN, D, AB_COLS), D ** -0.5),
        "ab_w_out": nrm((N_EVEN, MIX_WIDTH, D), MIX_WIDTH ** -0.5),
        "gla_w_gate": nrm((N_EVEN, GLA_RANK, GLA_HEADS * GLA_DK), GLA_RANK ** -0.5),
        "gla_b_gate": nrm((N_EVEN, GLA_HEADS * GLA_DK), 0.02),
        "gla_norm_g": gain((N_EVEN, GLA_DV)),
        "nsa_q_norm_g": gain((N_EVEN, NSA_DH)),
        "nsa_k_norm_g": gain((N_EVEN, NSA_DH)),
        "nsa_cmp_pos_k": nrm((N_EVEN, CMP_LEN, NSA_DH), 0.1),
        "nsa_cmp_pos_v": nrm((N_EVEN, CMP_LEN, NSA_DH), 0.1),
        "nsa_cmp_k_w1": nrm((N_EVEN, CMP_LEN * NSA_DH, NSA_DH), (CMP_LEN * NSA_DH) ** -0.5),
        "nsa_cmp_k_w2": nrm((N_EVEN, NSA_DH, NSA_DH), NSA_DH ** -0.5),
        "nsa_cmp_v_w1": nrm((N_EVEN, CMP_LEN * NSA_DH, NSA_DH), (CMP_LEN * NSA_DH) ** -0.5),
        "nsa_cmp_v_w2": nrm((N_EVEN, NSA_DH, NSA_DH), NSA_DH ** -0.5),
        "ml_w_in": nrm((N_ODD, D, ML_COLS), D ** -0.5),
        "ml_w_out": nrm((N_ODD, MIX_WIDTH, D), MIX_WIDTH ** -0.5),
        "ml_conv_w": nrm((N_ODD, ML_CONV, 2 * ML_HEADS * ML_DQK), ML_CONV ** -0.5),
        "ml_b_i": nrm((N_ODD, ML_HEADS), 0.1),
        "ml_b_f": 3.0 + 3.0 * jax.random.uniform(next(ks), (N_ODD, ML_HEADS), jnp.float32),
        "ml_norm_g": gain((N_ODD, ML_DV)),
    }

def reference(x, c, norm_mix_g, mod_mix_w, mod_mix_b, norm_mlp_g, mod_mlp_w, mod_mlp_b,
              mlp_w1, mlp_w2, ab_w_in, ab_w_out, gla_w_gate, gla_b_gate, gla_norm_g,
              nsa_q_norm_g, nsa_k_norm_g, nsa_cmp_pos_k, nsa_cmp_pos_v, nsa_cmp_k_w1, nsa_cmp_k_w2,
              nsa_cmp_v_w1, nsa_cmp_v_w2, ml_w_in, ml_w_out, ml_conv_w, ml_b_i, ml_b_f, ml_norm_g):
    for layer in range(DEPTH):
        shift, scale, gate = ada_mod(c, mod_mix_w[layer], mod_mix_b[layer])
        h = rmsnorm(x, norm_mix_g[layer]) * (1.0 + scale) + shift
        if layer % 2 == 0:
            e = layer // 2
            y = gla_nsa_mixer(h, ab_w_in[e], ab_w_out[e], gla_w_gate[e], gla_b_gate[e], gla_norm_g[e],
                              nsa_q_norm_g[e], nsa_k_norm_g[e], nsa_cmp_pos_k[e], nsa_cmp_pos_v[e],
                              nsa_cmp_k_w1[e], nsa_cmp_k_w2[e], nsa_cmp_v_w1[e], nsa_cmp_v_w2[e])
        else:
            o = layer // 2
            y = mlstm_mixer(h, ml_w_in[o], ml_w_out[o], ml_conv_w[o], ml_b_i[o], ml_b_f[o], ml_norm_g[o])
        x = x + gate * y
        shift, scale, gate = ada_mod(c, mod_mlp_w[layer], mod_mlp_b[layer])
        h = rmsnorm(x, norm_mlp_g[layer]) * (1.0 + scale) + shift
        x = x + gate * sqrelu_mlp(h, mlp_w1[layer], mlp_w2[layer])
    return x


_drawn_inputs = setup_inputs


def setup_inputs(seed=0):
    import zlib

    import numpy as np

    out = dict(_drawn_inputs(seed))
    spreads = {}
    factors = {'mod_mix_b': 2.709,
     'gla_b_gate': 8.0,
     'gla_norm_g': 3.959,
     'nsa_q_norm_g': 8.0,
     'nsa_k_norm_g': 8.0,
     'nsa_cmp_pos_k': 8.0,
     'nsa_cmp_pos_v': 8.0,
     'nsa_cmp_k_w1': 3.163,
     'nsa_cmp_k_w2': 3.173,
     'ml_b_i': 200.0,
     'ml_b_f': 23.864,
     'ml_norm_g': 3.442}
    for name, (base, spread) in spreads.items():
        noise = np.random.default_rng([zlib.crc32(name.encode()), seed]).standard_normal(out[name].shape)
        drawn = base * np.exp(spread * noise) if base else spread * noise
        out[name] = __import__('jax').numpy.asarray(drawn.astype(out[name].dtype))
    for name, factor in factors.items():
        out[name] = (out[name] * factor).astype(out[name].dtype)
    return out
```

```python
import concourse.bass as bass
from concourse import mybir
from contextlib import ExitStack

F32 = mybir.dt.float32
F32R = mybir.dt.float32r
ALU = mybir.AluOpType
ACT = mybir.ActivationFunctionType
AX = mybir.AxisListType

P = 128
D = 2048
T = 256
KC = D // P
TT = T // P
NEG = -1e30
EPS = 1e-6
GH, GDK, GDV, GTAU = 4, 128, 256, 16.0
GC = 64
NC_ = T // GC
NH, NG, DH = 16, 4, 64
NCMP = (T - 32) // 16 + 1
MH, MDK, MDV = 4, 256, 512
GLA_COLS = 2 * GH * GDK + 2 * GH * GDV + 16
AB_COLS = 5696
ML_COLS = 6152

P_PROJ0, P_OUT0, P_MLP0, P_PROJ1, P_OUT1, P_MLP1, P_END = 0, 12, 16, 48, 61, 65, 97

GQ, GK, GV, GR, NQ, CK, CV, SK, SV, WK, WV, ZT, GT = 0, 4, 8, 16, 24, 32, 34, 36, 38, 40, 42, 44, 45
MQ, MK, MV, MO, MG = 0, 8, 16, 32, 48

V_C, V_NMIX, V_NMLP, V_BG, V_GLAG, V_QG, V_KG, V_MLG, V_POSK = 0, 16, 48, 80, 84, 86, 87, 88, 92
V_CONV, V_POSV, V_BMIX, V_BMLP, V_N = 124, 188, 220, 316, 412
N_PARAMS, N_CONSTS = 23, 16


def trunk(nc, x, c, norm_mix_g, mod_mix_w, mod_mix_b, norm_mlp_g, mod_mlp_w, mod_mlp_b, mlp_w1, mlp_w2,
          ab_w_in, ab_w_out, gla_w_gate, gla_b_gate, gla_norm_g, nsa_q_norm_g, nsa_k_norm_g, nsa_cmp_pos_k,
          nsa_cmp_pos_v, nsa_cmp_k_w1, nsa_cmp_k_w2, nsa_cmp_v_w1, nsa_cmp_v_w2, ml_w_in, ml_w_out, ml_conv_w,
          ml_b_i, ml_b_f, ml_norm_g, out, upto=99):
    ctx = ExitStack()
    with ctx:
        arena = ctx.enter_context(nc.sbuf_tensor("arena", [P, 53200], F32))
        base = 16512

        def at(name, off, shape, dt=F32):
            return nc.alloc_sbuf_tensor_at(name, shape, dt, offset=base + off)

        O_X = 16384
        o_act = O_X
        o_prj = o_act + 32768
        o_raw = o_prj + 49152
        o_wh = o_raw + 32768
        o_wl = o_wh + 16384
        o_mr = o_wl + 16384
        o_acc = o_mr + 12288
        o_small = o_acc + 24576
        xT = at("xT", 0, [P, KC, T])
        act_hl = at("act_hl", o_act, [P, KC, 2, T], F32R)
        hid_hl = at("hid_hl", o_prj, [P, KC, 2, T], F32R)
        xproj = at("xproj", o_prj, [P, 48, T])
        raw = at("raw", o_raw, [P, 4, 4, 512])
        wh = at("wh", o_wh, [P, 4, 2, 512], F32R)
        wl = at("wl", o_wl, [P, 4, 2, 512], F32R)
        modring = at("modring", o_mr, [P, 2, 1536])
        acc = at("acc", o_acc, [P, 3 * D])
        o = o_small
        small = {}
        for name, shape in (("ident", [P, P]), ("ones", [P, P]), ("pair_ones", [P, P]), ("amask", [P, 3, P]),
                            ("cmask", [P, 2, TT, NCMP]), ("upper", [P, 2, P]), ("vecs", [P, V_N]),
                            ("modv", [P, 3, KC]), ("siluc", [P, KC]), ("std", [P, T]), ("gates", [P, T]),
                            ("w2k", [P, DH]), ("w2v", [P, DH]), ("brow", [1, 8]), ("eps", [P, 1])):
            n = 4
            for d in shape[1:]:
                n *= d
            small[name] = at(name, o, shape)
            o += (n + 31) // 32 * 32
        assert base + o <= 229344, base + o - 229344
        ident, ones, pair_ones, amask, cmask = (small[n] for n in ("ident", "ones", "pair_ones", "amask", "cmask"))
        upper, vecs, modv, siluc, std, gates = (small[n] for n in ("upper", "vecs", "modv", "siluc", "std", "gates"))
        w2k, w2v, brow, eps = (small[n] for n in ("w2k", "w2v", "brow", "eps"))
        xtok = at("xtok", o_act, [P, TT, D])
        startring = at("startring", o_prj, [P, 4, D])
        prow = at("prow", o_prj + 32768, [P, 4, P])
        sqb = at("sqb", o_prj + 32768, [P, 2, 4, T])
        xnb = at("xnb", o_prj + 40960, [P, 2, 4, T])
        relu = at("relu", o_prj + 32768, [P, 4, T])
        wgate = at("wgate", o_prj + 46 * 1024, [16, GH * GDK])
        K_ = 1024
        vt = at("vt", o_act, [P, TT, GH * GDV])
        la = at("la", o_act + 8 * K_, [P, GH, T])
        m13 = at("m13", o_act + 8 * K_, [P, GH, T])
        ep = at("ep", o_act + 12 * K_, [P, GH, T])
        u2 = at("u2", o_act + 12 * K_, [P, GH, P])
        u4 = at("u4", o_act + 14 * K_, [P, GH, P])
        ke = at("ke", o_act + 16 * K_, [P, GH, T])
        cum = at("cum", o_act + 20 * K_, [P, GH, T])
        seg = at("seg", o_act + 24 * K_, [P, GH, T])
        en = at("en", o_act + 28 * K_, [P, GH, T])
        et = at("et", o_prj + 44 * 1024, [P, GH, NC_])
        att = at("att", o_act + 16 * K_, [P, GH, 384])
        gstd = at("gstd", o_act + 22 * K_, [P, GH, T])
        gsq = at("gsq", o_act + 26 * K_, [P, 2, 2, T])
        sil = at("sil", o_act + 8 * K_, [P, 8, T])
        w1k = at("w1k", o_act, [P, 32, DH])
        w1v = at("w1v", o_act + 8 * K_, [P, 32, DH])
        nt = at("nt", o_act + 16 * K_, [P, 12, T])
        kcpk = at("kcpk", o_act + 16 * K_, [P, 32, 2, NCMP])
        kcpv = at("kcpv", o_act + 20 * K_, [P, 32, 2, NCMP])
        kdup = at("kdup", o_act + 24 * K_, [P, 2, NG, T])
        vsw = at("vsw", o_prj + CK * K_, [P, TT, 2, NG * DH])
        nso = at("nso", o_act, [P, 8, T])
        pb = at("pb", o_act + 8 * K_, [P, 2, 2, 384])
        pt = at("pt", o_act + 14 * K_, [P, 2, 2, 384])
        ptc = at("ptc", o_act + 20 * K_, [16, 2, T])
        sc = at("sc", o_prj + WV * K_, [P, TT, NH, NCMP])
        q_ = o_prj + SV * K_
        hk = at("hk", q_, [P, 2, 32])
        he = at("he", q_ + 256, [P, 2, 32])
        kcn = at("kcn", q_ + 512, [P, 32])
        kcs = at("kcs", q_ + 640, [P, 32])
        kcd = at("kcd", q_ + 768, [P, NG, NCMP])
        gt = at("gt", q_ + 1024, [P, TT, 48])
        cst = at("cst", q_ + 1408, [P, 3, TT, NH])
        vcm = at("vcm", o_prj + (SK) * K_, [16, NG * DH])
        hst = at("hst", o_prj + (SK + 1) * K_, [P, 2, 4, 2, 2])
        mvt = at("mvt", o_act, [P, TT, D])
        cva = at("cva", o_act, [P, 4, T])
        cvs = at("cvs", o_act + 16 * K_, [P, 8, T])
        dm = at("dm", o_act + 16 * K_, [P, 2, 384])
        sd = at("sd", o_act + 19 * K_, [P, 2, 384])
        mden = at("mden", o_act + 22 * K_, [P, T])
        mexp = at("mexp", o_act + 23 * K_, [P, T])
        msq = at("msq", o_act + 24 * K_, [P, 4, T])
        mg = at("mg", o_act + 28 * K_, [P, 3, TT, 8])
        ma = at("ma", o_act + 28 * K_ + 256, [P, TT, 4])
        brows = at("brows", o_act + 28 * K_ + 512, [4, 3, T])
        selh = at("selh", o_act + 31 * K_ + 512, [4, P])
        otok = at("otok", o_act, [P, TT, D])

        PS = ctx.enter_context(nc.psum_tensor("PS", [P, 8, 512], F32))

        def sem(name):
            return ctx.enter_context(nc.semaphore(name))

        raw_full = [sem(f"raw_full{s}") for s in range(4)]
        wh_ready = sem("wh_ready")
        wl_ready = sem("wl_ready")
        half_done = sem("half_done")
        psum_free = [sem("psum_free0"), sem("psum_free1")]
        act_ready = sem("act_ready")
        hid_ready = sem("hid_ready")
        mix_ready = sem("mix_ready")
        sq_done, hidh_done = sem("sq_done"), sem("hidh_done")
        start_full = [sem(f"start_full{s}") for s in range(4)]
        start_used = sem("start_used")
        mod_full = [sem("mod_full0"), sem("mod_full1")]
        mod_used = sem("mod_used")
        acc_clear, fold_done, mod_ready = sem("acc_clear"), sem("fold_done"), sem("mod_ready")
        params_in, x_in, consts_ready = sem("params_in"), sem("x_in"), sem("consts_ready")
        vecs_mm, vecs_ready, c_exp, silu_ready = sem("vecs_mm"), sem("vecs_ready"), sem("c_exp"), sem("silu_ready")
        xt_mm, xt_ready = sem("xt_mm"), sem("xt_ready")
        nsq_done, nstat_mm, nstd_done, xn_done, ah_done = (sem(n) for n in (
            "nsq_done", "nstat_mm", "nstd_done", "xn_done", "ah_done"))
        ot_mm, ot_ready, out_stored = sem("ot_mm"), sem("ot_ready"), sem("out_stored")
        g_names = ("wg_in", "gate_mm", "u", "nabs", "ln", "cum", "tmc", "ep", "en", "te", "keys", "vt_mm", "vt",
                   "seg", "att_mm", "att", "masked", "o_mm", "o", "osq", "st_mm", "std", "rexp", "res", "hh")
        g = {n: sem("g_" + n) for n in g_names}
        n_names = ("sq", "sq_mm", "std", "normed", "w1_in", "kdup_in", "kcp", "h_mm", "hexp", "hid", "kc_mm", "kcsq",
                   "kcsq_mm", "kcstd", "kcn", "kcd_in", "vc", "vsw_mm", "vsw", "gt_mm", "gexp", "cl_mm", "csub",
                   "cexp", "pc", "l_mm", "mx", "exp", "pn", "t_mm", "pt", "o_mm", "o", "hh")
        n_ = {n: sem("n_" + n) for n in n_names}
        m_names = ("cv", "cexp", "silu", "vt_mm", "vt", "gt_mm", "gcopy", "gabs", "gln", "lf", "b_mm", "rows", "a_mm",
                   "acol", "sel", "bc_mm", "dpre", "d", "em", "s_mm", "sd", "num_mm", "h", "hsq", "st_mm", "std", "oexp",
                   "hh", "res")
        m_ = {n: sem("m_" + n) for n in m_names}
        dve_chain, act_chain = sem("dve_chain"), sem("act_chain")

        block = ctx.enter_context(nc.Block())
        panels = {0: 12, 1: 16, 2: 48, 3: 65}.get(upto, P_END)
        done = [1 + (panels + 1) // 2, 1 + panels // 2]

        def banks(par):
            return PS[:, 2 * par:2 * par + 2, :].rearrange("p k (b t) -> p (k b) t", t=T)

        def raw_count(p, tail):
            return 16 * (p + 1 + (1 if tail else 0))

        def load_mod(eng, w, j, lo, width, slot, u):
            eng.wait_ge(mod_used, u + 1)
            eng.dma_start(modring[:, slot, 0:width], w[bass.ds(P * j, P), lo:lo + width]).then_inc(mod_full[slot], 16)

        def load_mod_row(eng, w, j, u):
            for k in range(4):
                load_mod(eng, w, j, 1536 * k, 1536, k % 2, u + k)

        def load_gate_row(eng, w, j, u):
            for k in range(2):
                load_mod(eng, w, j, 2 * D + 1024 * k, 1024, k, u + k)

        @block.sync
        def _(sp):
            def stage(src, col, p, s, cols=512):
                sp.wait_ge(wl_ready, 8 * p + 2 * s + 2)
                sp.dma_start(raw[:, s, :, 0:cols], rows_of(src, s, col, cols)).then_inc(raw_full[s], 16)

            def rows_of(src, s, col, cols):
                return src[512 * s:512 * s + 512, bass.ds(col, cols)].rearrange("(c p) n -> p c n", p=P)

            def store():
                for a in range(TT):
                    sp.wait_ge(ot_ready, 4 * a + 4)
                    sp.dma_start(out[0, P * a:P * a + P, :], otok[:, a, :]).then_inc(out_stored, 16)
                sp.wait_ge(out_stored, 16 * TT)

            sp.dma_start(xtok[:, :, :], x[0].rearrange("(a p) n -> p a n", p=P)).then_inc(x_in, 16)
            with sp.Fori(0, 8) as i:
                for k in range(4):
                    sp.wait_ge(start_used, 4 * i + k + 1)
                    sp.dma_start(startring[:, k, :], mod_mix_w[0][bass.ds(P * (2 * i + k // 2), P),
                                 D * (k % 2):D * (k % 2) + D]).then_inc(start_full[k], 16)
            sp.wait_ge(start_used, 33)
            sp.dma_start(startring[:, 0, :], mod_mix_w[0][15 * P:16 * P, 2 * D:3 * D]).then_inc(start_full[0], 16)

            w_in = ab_w_in[0]
            with sp.Fori(0, 3) as i:
                for a in range(2):
                    for s in range(4):
                        stage(w_in, 512 * (2 * i + a), 2 * i + a, s)
            with sp.Fori(0, 2) as i:
                for a in range(2):
                    for s in range(4):
                        stage(w_in, GLA_COLS + 512 * (2 * i + a), 6 + 2 * i + a, s)
            for s in range(4):
                stage(w_in, GLA_COLS + 2048, 10, s)
            for s in range(4):
                sp.wait_ge(wl_ready, 8 * 11 + 2 * s + 2)
                for b, col in ((0, GLA_COLS - 16), (1, AB_COLS - P)):
                    sp.dma_start(raw[:, s, :, P * b:P * b + P], rows_of(w_in, s, col, P)).then_inc(raw_full[s], 16)
            if upto < 1:
                for s in range(2):
                    stage(ab_w_out[0], 0, P_OUT0, s)
                return store()
            for s in range(2):
                stage(ab_w_out[0], 0, P_OUT0, s)
            sp.wait_ge(act_ready, 4)
            sp.dma_start(wgate[:, :], gla_w_gate[0]).then_inc(g["wg_in"], 16)
            for s in range(2, 4):
                stage(ab_w_out[0], 0, P_OUT0, s)
            for a in range(1, 4):
                for s in range(4):
                    stage(ab_w_out[0], 512 * a, P_OUT0 + a, s)

            def mlp(l, p0):
                def quarter(q):
                    for a in range(8):
                        for s in range(4):
                            if a < 4:
                                stage(mlp_w1[l], D * q + 512 * a, p0 + 8 * q + a, s)
                            else:
                                sp.wait_ge(wl_ready, 8 * (p0 + 8 * q + a) + 2 * s + 2)
                                src = mlp_w2[l][bass.ds(D * q + 512 * s, 512), 512 * (a - 4):512 * (a - 3)]
                                sp.dma_start(raw[:, s, :, :], src.rearrange("(c p) n -> p c n", p=P))\
                                  .then_inc(raw_full[s], 16)
                with sp.Fori(0, 4) as q:
                    quarter(q)
            if upto < 2:
                for s in range(2):
                    stage(mlp_w1[0], 0, P_MLP0, s)
                return store()
            mlp(0, P_MLP0)
            if upto < 3:
                for s in range(2):
                    stage(ml_w_in[0], 0, P_PROJ1, s)
                return store()
            with sp.Fori(0, 6) as i:
                for a in range(2):
                    for s in range(4):
                        stage(ml_w_in[0], 512 * (2 * i + a), P_PROJ1 + 2 * i + a, s)
            for s in range(4):
                stage(ml_w_in[0], ML_COLS - P, P_PROJ1 + 12, s, P)
            for s in range(2):
                stage(ml_w_out[0], 0, P_OUT1, s)
            for s in range(2, 4):
                stage(ml_w_out[0], 0, P_OUT1, s)
            for a in range(1, 4):
                for s in range(4):
                    stage(ml_w_out[0], 512 * a, P_OUT1 + a, s)
            if upto < 4:
                for s in range(2):
                    stage(mlp_w1[1], 0, P_MLP1, s)
                return store()
            mlp(1, P_MLP1)
            store()

        @block.scalar
        def _(act):
            chain = [0]

            def link(ins):
                chain[0] += 1
                ins.then_inc(act_chain, 1)
                act.wait_ge(act_chain, chain[0])

            fn = nc.scalar.activation

            def result():
                for s_, v in zip(psum_free, done):
                    act.wait_ge(s_, v)
                for k in range(8):
                    act.wait_ge(ot_mm, k + 1)
                    fn(otok[:, k // 4, 512 * (k % 4):512 * (k % 4) + 512], PS[:, k % 4, :], ACT.Copy).then_inc(ot_ready, 1)

            n_params = [0]

            def par(dst, src):
                n_params[0] += 1
                act.dma_start(dst, src).then_inc(params_in, 16)
            par(prow[0:16, 0, :], c[0].rearrange("(m p) -> m p", p=P))
            par(prow[16:48, 0, :], norm_mix_g.rearrange("l (m p) -> (l m) p", p=P))
            par(prow[48:80, 0, :], norm_mlp_g.rearrange("l (m p) -> (l m) p", p=P))
            par(prow[80:84, 0, :], gla_b_gate[0].rearrange("(m p) -> m p", p=P))
            par(prow[84:86, 0, :], gla_norm_g[0].rearrange("(m p) -> m p", p=P))
            for k in range(2):
                par(prow[86:87, 0, DH * k:DH * k + DH], nsa_q_norm_g)
                par(prow[87:88, 0, DH * k:DH * k + DH], nsa_k_norm_g)
                par(prow[92:124, 0, DH * k:DH * k + DH], nsa_cmp_pos_k[0])
                par(prow[64:96, 1, DH * k:DH * k + DH], nsa_cmp_pos_v[0])
                par((w2k, w2v)[0][DH * k:DH * k + DH, :], nsa_cmp_k_w2[0])
                par((w2k, w2v)[1][DH * k:DH * k + DH, :], nsa_cmp_v_w2[0])
            par(prow[88:92, 0, :], ml_norm_g[0].rearrange("(m p) -> m p", p=P))
            par(prow[0:64, 1, :], ml_conv_w[0].rearrange("j (m p) -> (j m) p", p=P))
            par(prow[0:96, 2, :], mod_mix_b.rearrange("l (m p) -> (l m) p", p=P))
            par(prow[0:96, 3, :], mod_mlp_b.rearrange("l (m p) -> (l m) p", p=P))
            par(brow[0:1, 0:4], ml_b_i)
            par(brow[0:1, 4:8], ml_b_f)
            assert n_params[0] == N_PARAMS

            act.wait_ge(vecs_mm, 1)
            fn(vecs[:, 0:124], PS[:, 4, 0:124], ACT.Copy)
            fn(vecs[:, 124:220], PS[:, 4, 128:224], ACT.Copy)
            fn(vecs[:, 220:316], PS[:, 4, 256:352], ACT.Copy)
            fn(vecs[:, 316:412], PS[:, 4, 384:480], ACT.Copy).then_inc(vecs_ready, 1)
            act.wait_ge(vecs_ready, 1)
            fn(siluc[:, :], vecs[:, V_C:V_C + KC], ACT.Exp, scale=-1.0).then_inc(c_exp, 1)
            for k in range(8):
                act.wait_ge(xt_mm, k + 1)
                fn(xT[:, 2 * k:2 * k + 2, :].rearrange("p b t -> p (b t)"), PS[:, k % 4, :], ACT.Copy).then_inc(xt_ready, 1)

            def half(p, h, tail=False, cols=512):
                s = h // 2
                if h % 2 == 0:
                    act.wait_ge(raw_full[s], raw_count(p, tail))
                act.wait_ge(half_done, 8 * p + h + 1)
                fn(wh[:, h % 4, :, 0:cols], raw[:, s, 2 * (h % 2):2 * (h % 2) + 2, 0:cols], ACT.Copy)\
                    .then_inc(wh_ready, 1)

            def segment(p, before=None, after=None, tail=False, cols=512, tail2=None, cols2=512):
                tail2 = tail if tail2 is None else tail2
                for h in range(4, 8):
                    if before:
                        before(h)
                    half(p, h, tail, cols)
                for h in range(4):
                    half(p + 1, h, tail2, cols2)

            def panel_done(p):
                act.wait_ge(half_done, 8 * p + 12)

            def evac_proj(p, par, blk, nb=4):
                panel_done(p)
                fn(xproj[:, bass.ds(blk, nb), :], banks(par)[:, 0:nb, :], ACT.Copy).then_inc(psum_free[par], 1)

            def norm_squares(n, xready):
                for s_, v in xready:
                    act.wait_ge(s_, v)
                for k in range(4):
                    if k >= 2:
                        act.wait_ge(nstat_mm, 4 * n + k - 1)
                    fn(sqb[:, k % 2], xT[:, 4 * k:4 * k + 4, :], ACT.Square).then_inc(nsq_done, 1)

            def norm(n, xready=None):
                if xready:
                    norm_squares(n, xready)
                act.wait_ge(nstat_mm, 4 * n + 4)
                fn(std[:, :], PS[:, 5, 0:T], ACT.Sqrt, bias=eps[:, :], scale=1.0 / D).then_inc(nstd_done, 1)
                act.wait_ge(mod_ready, n + 1)
                for k in range(4):
                    act.wait_ge(xn_done, 4 * n + k + 1)
                    for b in range(4):
                        m = 4 * k + b
                        ins = fn(xnb[:, k % 2, b, :], xnb[:, k % 2, b, :], ACT.Identity,
                                 scale=modv[:, 1, m:m + 1], bias=modv[:, 0, m:m + 1])
                    link(ins)
                    fn(act_hl[:, 4 * k:4 * k + 4, 0, :], xnb[:, k % 2], ACT.Copy).then_inc(ah_done, 1)

            norm_squares(0, [(xt_ready, 8)])
            act.wait_ge(consts_ready, N_CONSTS)
            norm(0)
            for h in range(4):
                half(0, h)
            with act.Fori(0, 5) as i:
                for a in range(2):
                    segment(2 * i + a)
                    evac_proj(2 * i + a, a, 8 * i + 4 * a)
            segment(10, tail=False, tail2=True, cols2=256)
            evac_proj(10, 0, 40)
            segment(11, tail=True, cols=256)
            evac_proj(11, 1, ZT, 2)
            if upto < 1:
                return result()
            for h in range(GH):
                act.wait_ge(g["gate_mm"], 1)
                ins = fn(la[:, h, :], PS[:, 4 + h // 2, T * (h % 2):T * (h % 2) + T], ACT.Identity,
                         bias=vecs[:, V_BG + h:V_BG + h + 1])
            ins.then_inc(g["u"], 1)
            for k in range(4):
                act.wait_ge(g["vt_mm"], k + 1)
                fn(vt[:, k // 2, 512 * (k % 2):512 * (k % 2) + 512], PS[:, k, :], ACT.Copy).then_inc(g["vt"], 1)
            act.wait_ge(g["nabs"], 1)
            link(fn(ke[:, :, :], ke[:, :, :], ACT.Exp))
            fn(ke[:, :, :], ke[:, :, :], ACT.Ln, bias=ones[:, 0:1]).then_inc(g["ln"], 1)
            act.wait_ge(g["cum"], 1)
            fn(ep[:, :, :], cum[:, :, :], ACT.Exp, scale=1.0 / GTAU).then_inc(g["ep"], 1)
            fn(et[:, :, :], cum[:, :, GC - 1::GC], ACT.Exp, scale=1.0 / GTAU)
            fn(en[:, :, :], cum[:, :, :], ACT.Exp, scale=-1.0 / GTAU).then_inc(g["en"], 1)
            act.wait_ge(g["tmc"], 1)
            fn(seg[:, :, :], seg[:, :, :], ACT.Exp, scale=1.0 / GTAU).then_inc(g["te"], 1)
            for h in range(GH):
                act.wait_ge(g["att_mm"], h + 1)
                fn(att[:, h, :], PS[:, 4 + h, 0:384], ACT.Copy, scale=GDK ** -0.5).then_inc(g["att"], 1)
            for h in range(GH):
                act.wait_ge(g["o_mm"], h + 1)
                if h >= 2:
                    act.wait_ge(g["st_mm"], h - 1)
                fn(gsq[:, h % 2], PS[:, h, :].rearrange("p (v t) -> p v t", v=2), ACT.Square).then_inc(g["osq"], 1)
                fn(xproj[:, GV + 2 * h:GV + 2 * h + 2, :], PS[:, h, :].rearrange("p (v t) -> p v t", v=2),
                   ACT.Copy).then_inc(g["o"], 1)
            fn(sil[:, :, :], xproj[:, GR:GR + 8, :], ACT.Exp, scale=-1.0).then_inc(g["rexp"], 1)
            act.wait_ge(g["st_mm"], 4)
            fn(gstd[:, :, :], PS[:, 4:6, :].rearrange("p k (b t) -> p (k b) t", t=T), ACT.Sqrt, bias=eps[:, :],
               scale=1.0 / GDV).then_inc(g["std"], 1)
            act.wait_ge(g["res"], 1)
            for k in range(2):
                fn(hid_hl[:, 4 * k:4 * k + 4, 0, :], xproj[:, GR + 4 * k:GR + 4 * k + 4, :], ACT.Copy)\
                    .then_inc(g["hh"], 1)
            fn(nt[:, 0:8, :], xproj[:, NQ:NQ + 8, :], ACT.Square)
            fn(nt[:, 8:10, :], xproj[:, SK:SK + 2, :], ACT.Square)
            fn(nt[:, 10:12, :], xproj[:, WK:WK + 2, :], ACT.Square).then_inc(n_["sq"], 1)
            act.wait_ge(n_["sq_mm"], 1)
            fn(nt[:, :, :], PS[:, 0:6, :].rearrange("p k (b t) -> p (k b) t", t=T), ACT.Sqrt, bias=eps[:, :],
               scale=1.0 / DH).then_inc(n_["std"], 1)
            act.wait_ge(n_["h_mm"], 1)
            fn(he[:, :, 0:30], PS[:, 4:6, 0:30], ACT.Exp, scale=-1.0)
            fn(hk[:, :, 0:30], PS[:, 4:6, 0:30], ACT.Copy).then_inc(n_["hexp"], 1)
            act.wait_ge(n_["vsw_mm"], 1)
            act.wait_ge(n_["kcp"], 1)
            for k in range(2):
                fn(vsw[:, k], PS[:, 6 + k, :].rearrange("p (b d) -> p b d", b=2), ACT.Copy).then_inc(n_["vsw"], 1)
            act.wait_ge(n_["gt_mm"], 1)
            fn(gt[:, :, :], PS[:, 2, 0:256].rearrange("p (a f) -> p a f", a=2)[:, :, 80:128], ACT.Exp, scale=-1.0)\
                .then_inc(n_["gexp"], 1)
            act.wait_ge(n_["kc_mm"], 1)
            fn(kcs[:, 0:30], PS[:, 4, 64:94], ACT.Square).then_inc(n_["kcsq"], 1)
            fn(kcn[:, 0:30], PS[:, 4, 64:94], ACT.Copy)
            act.wait_ge(n_["kdup_in"], 128)
            fn(vcm[0:NCMP, :].rearrange("n (b g d) -> n g b d", b=2, g=2),
               PS[0:NCMP, 0:2, 0:P].rearrange("n g (b d) -> n g b d", b=2), ACT.Copy).then_inc(n_["vc"], 1)
            act.wait_ge(n_["kcsq_mm"], 1)
            fn(kcs[:, 0:30], PS[:, 5, 128:158], ACT.Sqrt, bias=eps[:, :], scale=1.0 / DH).then_inc(n_["kcstd"], 1)
            act.wait_ge(n_["csub"], 1)
            fn(sc[:, :, :, :], sc[:, :, :, :], ACT.Exp, scale=DH ** -0.5).then_inc(n_["cexp"], 1)
            for h in range(NH):
                b = h % 2
                act.wait_ge(n_["mx"], h + 1)
                for br in range(2):
                    for tt, (lo, hi) in enumerate(((0, P), (P, 384))):
                        ins = fn(pb[:, b, br, lo:hi], pb[:, b, br, lo:hi], ACT.Exp, scale=DH ** -0.5,
                                 bias=hst[:, b, 1, br, tt:tt + 1], accum_out=hst[:, b, 2, br, tt:tt + 1])
                ins.then_inc(n_["exp"], 1)
                act.wait_ge(n_["t_mm"], h + 1)
                if h >= 2:
                    act.wait_ge(n_["o_mm"], h - 1)
                fn(pt[:, b], PS[:, 4:6, 0:384], ACT.Copy)
                fn(ptc[0:NCMP, b, :].rearrange("n (a t) -> n a t", a=TT), PS[0:NCMP, 4:6, 384:512], ACT.Copy).then_inc(n_["pt"], 1)
            for k in range(2):
                act.wait_ge(n_["o"], 4 * k + 4)
                fn(hid_hl[:, 8 + 4 * k:12 + 4 * k, 0, :], nso[:, 4 * k:4 * k + 4, :], ACT.Copy).then_inc(n_["hh"], 1)

            for a in range(4):
                segment(P_OUT0 + a, tail=True)

            def mlp(l, p0, last):
                def quarter(q, final=False):
                    for a in range(8):
                        n = 16 * l + 4 * q + a

                        def before(h, a=a, n=n):
                            if 1 <= a <= 4 and h == 6:
                                act.wait_ge(sq_done, n)
                                fn(hid_hl[:, 4 * (a - 1):4 * a, 0, :], relu[:, :, :], ACT.Copy).then_inc(hidh_done, 1)
                        if final and a == 7:
                            for h in range(4, 8):
                                half(p0 + 8 * q + a, h, True)
                        else:
                            segment(p0 + 8 * q + a, before, tail=True)
                        if a < 4:
                            panel_done(p0 + 8 * q + a)
                            act.wait_ge(hid_ready, n + 1)
                            par = (p0 + a) % 2
                            fn(relu[:, :, :], banks(par), ACT.Relu).then_inc(psum_free[par], 1)
                with act.Fori(0, 3 if last else 4) as q:
                    quarter(q)
                if last:
                    quarter(3, True)

            if upto < 2:
                return result()
            norm(1, [(psum_free[0], P_MLP0 // 2 + 1), (psum_free[1], P_MLP0 // 2 + 1)])
            mlp(0, P_MLP0, False)
            if upto < 3:
                return result()
            norm(2, [(psum_free[0], P_PROJ1 // 2 + 1), (psum_free[1], P_PROJ1 // 2 + 1)])
            with act.Fori(0, 5) as i:
                for a in range(2):
                    segment(P_PROJ1 + 2 * i + a, tail=True)
                    evac_proj(P_PROJ1 + 2 * i + a, a, 8 * i + 4 * a)
            segment(P_PROJ1 + 10, tail=True)
            evac_proj(P_PROJ1 + 10, 0, 40)
            segment(P_PROJ1 + 11, tail=True, cols2=P)
            evac_proj(P_PROJ1 + 11, 1, 44)
            segment(P_PROJ1 + 12, tail=True, cols=P)
            panel_done(P_PROJ1 + 12)
            fn(gates[:, :], PS[:, 0, 0:T], ACT.Copy).then_inc(psum_free[0], 1)
            for k in range(2):
                act.wait_ge(m_["cv"], 2 * k + 2)
                fn(cvs[:, :, :], xproj[:, 8 * k:8 * k + 8, :], ACT.Exp, scale=-1.0).then_inc(m_["cexp"], 1)
                act.wait_ge(m_["silu"], k + 1)
            for k in range(8):
                act.wait_ge(m_["vt_mm"], k + 1)
                fn(mvt[:, k // 4, 512 * (k % 4):512 * (k % 4) + 512], PS[:, k % 4, :], ACT.Copy).then_inc(m_["vt"], 1)
            act.wait_ge(m_["gt_mm"], 1)
            fn(mg[:, 0], PS[:, 4, 0:256].rearrange("p (a f) -> p a f", a=2)[:, :, 120:128], ACT.Copy)\
                .then_inc(m_["gcopy"], 1)
            act.wait_ge(m_["gabs"], 1)
            link(fn(mg[:, 2, :, 4:8], mg[:, 1, :, 4:8], ACT.Exp))
            fn(mg[:, 2, :, 4:8], mg[:, 2, :, 4:8], ACT.Ln, bias=ones[:, 0:1]).then_inc(m_["gln"], 1)
            act.wait_ge(m_["a_mm"], 1)
            fn(ma[:, :, :], PS[:, 6, 0:16].rearrange("p (a f) -> p a f", a=2)[:, :, 0:4], ACT.Copy)\
                .then_inc(m_["acol"], 1)
            for h in range(MH):
                b = h % 2
                act.wait_ge(m_["dpre"], h + 1)
                if h == 0:
                    act.wait_ge(m_["acol"], 1)
                fn(dm[:, b, 0:256], dm[:, b, 0:256], ACT.Exp, bias=ma[:, 0, h:h + 1])
                fn(dm[:, b, 256:384], dm[:, b, 256:384], ACT.Exp, bias=ma[:, 1, h:h + 1]).then_inc(m_["d"], 1)
                fn(mexp[:, :], PS[:, 5, T:2 * T], ACT.Exp, scale=-1.0).then_inc(m_["em"], 1)
                act.wait_ge(m_["h"], h + 1)
                fn(msq[:, :, :], xproj[:, MV + 4 * h:MV + 4 * h + 4, :], ACT.Square).then_inc(m_["hsq"], 1)
                act.wait_ge(m_["st_mm"], h + 1)
                fn(std[:, :], PS[:, 7, 0:T], ACT.Sqrt, bias=eps[:, :], scale=1.0 / MDV).then_inc(m_["std"], 1)
                fn(msq[:, :, :], xproj[:, MO + 4 * h:MO + 4 * h + 4, :], ACT.Exp, scale=-1.0).then_inc(m_["oexp"], 1)
                act.wait_ge(m_["res"], h + 1)
            for h in range(MH):
                fn(hid_hl[:, 4 * h:4 * h + 4, 0, :], xproj[:, MO + 4 * h:MO + 4 * h + 4, :], ACT.Copy)\
                    .then_inc(m_["hh"], 1)
            for a in range(4):
                segment(P_OUT1 + a, tail=True)
            if upto < 4:
                return result()
            norm(3, [(psum_free[0], 34), (psum_free[1], 33)])
            mlp(1, P_MLP1, True)
            result()

        @block.gpsimd
        def _(pool):
            pool_n = [0]

            def step(ins):
                pool_n[0] += 1
                ins.then_inc(consts_ready, 1)
                pool.wait_ge(consts_ready, pool_n[0])
            ge, gt_ = ALU.is_ge, ALU.is_gt
            step(nc.gpsimd.memset(acc[:, :], 0.0))
            step(nc.gpsimd.memset(ident[:, :], 0.0))
            step(nc.gpsimd.affine_select(out=ident[:, :], in_=ident[:, :], compare_op=ALU.not_equal, fill=1.0,
                                         base=0, pattern=[[-1, P]], channel_multiplier=1))
            step(nc.gpsimd.memset(ones[:, :], 1.0))
            step(nc.gpsimd.memset(eps[:, :], EPS))
            step(nc.gpsimd.memset(pair_ones[:, :], 0.0))
            for k in range(2):
                step(nc.gpsimd.memset(pair_ones[DH * k:DH * k + DH, DH * k:DH * k + DH], 1.0))
            step(nc.gpsimd.memset(amask[:, :, :], 0.0))
            step(nc.gpsimd.affine_select(out=amask[:, 0::2, :], in_=amask[:, 0::2, :], compare_op=ge, fill=NEG,
                                         base=0, pattern=[[0, 2], [-1, P]], channel_multiplier=1))
            for k, (inside, outside) in enumerate(((0.0, NEG), (1.0, 0.0))):
                step(nc.gpsimd.memset(cmask[:, k], inside))
                step(nc.gpsimd.affine_select(out=cmask[:, k], in_=cmask[:, k], compare_op=ge, fill=outside,
                                             base=-31, pattern=[[P, TT], [-16, NCMP]], channel_multiplier=1))
            step(nc.gpsimd.memset(upper[:, :, :], 1.0))
            step(nc.gpsimd.affine_select(out=upper[:, 0, :], in_=upper[:, 0, :], compare_op=ge, fill=0.0,
                                         base=0, pattern=[[1, P]], channel_multiplier=-1))
            assert pool_n[0] == N_CONSTS
            with pool.Fori(0, 15) as i:
                load_gate_row(pool, mod_mix_w[0], i, 2 * i)
            pool.wait_ge(fold_done, 2)
            nc.gpsimd.memset(acc[:, :], 0.0).then_inc(acc_clear, 1)
            with pool.Fori(0, 6) as i:
                load_mod_row(pool, mod_mlp_w[0], i, 30 + 4 * i)
            if upto < 1:
                return
            pool.wait_ge(half_done, 4 + 8 * P_OUT0)
            nc.gpsimd.memset(seg[:, :, :], 1.0).then_inc(g["seg"], 1)
            pool.wait_ge(g["seg"], 1)
            nc.gpsimd.memset(seg[:, :, 0::GC], 0.0).then_inc(g["seg"], 1)

            def mlp0_row(j):
                load_mod_row(pool, mod_mlp_w[0], j, 30 + 4 * j)
            mlp0_row(6)
            mlp0_row(7)
            for h in range(GH):
                pool.wait_ge(g["att"], h + 1)
                v = att[:, h, :].rearrange("p (b t) -> p b t", t=P)[:, 0::2, :]
                nc.gpsimd.affine_select(out=v, in_=v, compare_op=ge, fill=0.0, base=0, pattern=[[0, 2], [1, P]],
                                        channel_multiplier=-1).then_inc(g["masked"], 1)
            pool.wait_ge(g["res"], 1)
            for k in range(2):
                for w, src in ((w1k, nsa_cmp_k_w1), (w1v, nsa_cmp_v_w1)):
                    pool.dma_start(w[DH * k:DH * k + DH, :, :], src[0].rearrange("(l d) e -> d l e", d=DH))\
                        .then_inc(n_["w1_in"], 16)
            mlp0_row(8)
            pool.wait_ge(n_["normed"], 2)
            for br, blk in ((0, SK), (1, WK)):
                for gp in range(2):
                    for k in range(2):
                        pool.dma_start(kdup[DH * k:DH * k + DH, br, gp::2, :], xproj[DH * gp:DH * gp + DH, blk:blk + 2, :])\
                            .then_inc(n_["kdup_in"], 16)
            mlp0_row(9)
            pool.wait_ge(n_["kcn"], 1)
            for gp in range(2):
                for k in range(2):
                    pool.dma_start(kcd[DH * k:DH * k + DH, gp::2, :],
                                   kcn[DH * gp:DH * gp + DH, 0:30].rearrange("p (b n) -> p b n", b=2))\
                        .then_inc(n_["kcd_in"], 16)
            for j in range(10, 16):
                mlp0_row(j)
            if upto < 2:
                return
            pool.wait_ge(fold_done, 3)
            nc.gpsimd.memset(acc[:, :], 0.0).then_inc(acc_clear, 1)
            if upto < 3:
                return
            nc.gpsimd.memset(amask[:, :, :], 0.0).then_inc(acc_clear, 1)
            pool.wait_ge(acc_clear, 3)
            nc.gpsimd.affine_select(out=amask[:, 0::2, :], in_=amask[:, 0::2, :], compare_op=ge, fill=NEG,
                                    base=0, pattern=[[0, 2], [1, P]], channel_multiplier=-1).then_inc(acc_clear, 1)
            with pool.Fori(0, 16) as i:
                load_mod_row(pool, mod_mix_w[1], i, 94 + 4 * i)
            pool.wait_ge(fold_done, 4)
            nc.gpsimd.memset(acc[:, :], 0.0).then_inc(acc_clear, 1)
            with pool.Fori(0, 16) as i:
                load_mod_row(pool, mod_mlp_w[1], i, 158 + 4 * i)

        @block.vector
        def _(dve):
            V = nc.vector
            chain = [0]

            def link(ins):
                chain[0] += 1
                ins.then_inc(dve_chain, 1)
                dve.wait_ge(dve_chain, chain[0])

            dve.sem_inc(wl_ready, 8)
            dve.sem_inc(start_used, 4)
            dve.sem_inc(mod_used, 2)
            dve.sem_inc(hid_ready, 1)
            dve.wait_ge(c_exp, 1)
            link(V.tensor_scalar(siluc[:, :], siluc[:, :], 1.0, None, ALU.add))
            link(V.reciprocal(siluc[:, :], siluc[:, :]))
            link(V.tensor_tensor(siluc[:, :], siluc[:, :], vecs[:, V_C:V_C + KC], ALU.mult))

            def accumulate(piece, j, lo, width):
                a = acc[:, lo:lo + width]
                return V.scalar_tensor_tensor(a, piece, siluc[:, bass.ds(j, 1)], a, ALU.mult, ALU.add)

            dve.wait_ge(consts_ready, N_CONSTS)
            with dve.Fori(0, 8) as i:
                for k in range(4):
                    dve.wait_ge(start_full[k], 16 * i + 16)
                    dve.wait_ge(start_used, 4 * i + k + 3)
                    accumulate(startring[:, k, :], 2 * i + k // 2, D * (k % 2), D).then_inc(start_used, 1)
            dve.wait_ge(start_full[0], 16 * 9)
            accumulate(startring[:, 0, :], 15, 2 * D, D).then_inc(start_used, 1)

            def mod(j, lo, width, slot, uh, u, per_row):
                dve.wait_ge(mod_full[slot], 16 * uh + 16)
                dve.wait_ge(mod_used, u - per_row + 3)
                accumulate(modring[:, slot, 0:width], j, lo, width).then_inc(mod_used, 1)

            def mod_pieces(j, u):
                return [lambda k=k: mod(j, 1536 * k, 1536, k % 2, uh_of(u, k), uu(u, k), 4) for k in range(4)]

            def uu(u, k):
                return u[0] + k

            def uh_of(u, k):
                return u[1] + k // 2

            def gate_pieces(j, row):
                return [lambda k=k: mod(j, 2 * D + 1024 * k, 1024, k, row, 2 * row + k, 2) for k in range(2)]

            def half(p, h, cols=512):
                dve.wait_ge(wh_ready, 8 * p + h + 1)
                V.tensor_tensor(wl[:, h % 4, :, 0:cols], raw[:, h // 2, 2 * (h % 2):2 * (h % 2) + 2, 0:cols],
                                wh[:, h % 4, :, 0:cols].bitcast(F32), ALU.subtract).then_inc(wl_ready, 1)

            def segment(p, pieces=(), before=None, cols=512, cols2=512):
                pieces = list(pieces)
                for k in range(8):
                    h = (k + 4) % 8
                    if before:
                        before(k)
                    if k < 4:
                        half(p, h, cols)
                    else:
                        half(p + 1, h, cols2)
                    if pieces and k >= 2:
                        pieces.pop(0)()
                for piece in pieces:
                    piece()

            def fold(n, k, lo, hi, bias, gcol, panels_out=()):
                for s_, v in zip(psum_free, panels_out):
                    dve.wait_ge(s_, v)
                dve.wait_ge(fold_done, k)
                dst = modv[:, :, :].rearrange("p s m -> p (s m)")[:, lo:hi]
                ins = V.tensor_tensor(dst, PS[:, 6, lo:hi], vecs[:, bias + lo:bias + hi], ALU.add)
                link(ins)
                if gcol is not None:
                    V.scalar_tensor_tensor(modv[:, 1, :], modv[:, 1, :], 1.0, vecs[:, gcol:gcol + KC], ALU.add, ALU.mult)\
                        .then_inc(mod_ready, 1)

            def norm(n):
                dve.wait_ge(nstd_done, n + 1)
                link(V.reciprocal(std[:, :], std[:, :]))
                rb = std[:, :].unsqueeze(1).broadcast_to([P, 4, T])

                def xn(k):
                    if k >= 2:
                        dve.wait_ge(act_ready, 4 * n + k - 1)
                    V.tensor_tensor(xnb[:, k % 2], xT[:, 4 * k:4 * k + 4, :], rb, ALU.mult).then_inc(xn_done, 1)

                def al(k):
                    dve.wait_ge(ah_done, 4 * n + k + 1)
                    V.tensor_tensor(act_hl[:, 4 * k:4 * k + 4, 1, :], xnb[:, k % 2],
                                    act_hl[:, 4 * k:4 * k + 4, 0, :].bitcast(F32), ALU.subtract).then_inc(act_ready, 1)
                xn(0)
                xn(1)
                for k in range(4):
                    al(k)
                    if k + 2 < 4:
                        xn(k + 2)

            def evac_add(p, ph, par, col):
                dve.wait_ge(half_done, 8 * p + 12)
                dve.wait_ge(psum_free[par], ph - 2)
                for b in range(4):
                    xb = xT[:, 4 * col + b, :]
                    ins = V.scalar_tensor_tensor(xb, banks(par)[:, b, :], modv[:, 2, 4 * col + b:4 * col + b + 1], xb,
                                                 ALU.mult, ALU.add)
                ins.then_inc(psum_free[par], 1)

            fold(0, 1, 0, 2 * KC, V_BMIX, V_NMIX)
            dve.wait_ge(xt_ready, 8)
            norm(0)
            for h in range(4):
                half(0, h)
            with dve.Fori(0, 3) as i:
                segment(2 * i, sum((gate_pieces(5 * i + j, 5 * i + j) for j in range(3)), []))
                segment(2 * i + 1, sum((gate_pieces(5 * i + j, 5 * i + j) for j in range(3, 5)), []))
            dve.wait_ge(acc_clear, 1)
            with dve.Fori(0, 2) as i:
                segment(6 + 2 * i, mod_pieces(2 * i, (30 + 8 * i, 15 + 4 * i)))
                segment(7 + 2 * i, mod_pieces(2 * i + 1, (34 + 8 * i, 17 + 4 * i)))
            fold(0, 2, 2 * KC, 3 * KC, V_BMIX, None)
            segment(10, mod_pieces(4, (46, 23)), cols2=256)
            segment(11, mod_pieces(5, (50, 25)), cols=256)
            if upto < 1:
                dve.wait_ge(psum_free[1], 7)
                return

            def mods(j):
                for piece in mod_pieces(j, (30 + 4 * j, 15 + 2 * j)):
                    piece()
            dve.wait_ge(g["u"], 1)
            V.scalar_tensor_tensor(ke[:, :, :], la[:, :, :], -1.0, la[:, :, :], ALU.mult, ALU.min)\
                .then_inc(g["nabs"], 1)
            dve.wait_ge(g["ln"], 1)
            link(V.scalar_tensor_tensor(la[:, :, :], la[:, :, :], 0.0, ke[:, :, :], ALU.min, ALU.subtract))
            dve.wait_ge(g["seg"], 2)
            V.tensor_tensor_scan(cum[:, :, :].rearrange("p h t -> p (h t)"), seg[:, :, :].rearrange("p h t -> p (h t)"),
                                 la[:, :, :].rearrange("p h t -> p (h t)"), 0.0, ALU.mult, ALU.add).then_inc(g["cum"], 1)
            dve.wait_ge(g["cum"], 1)
            c4 = cum[:, :, :].rearrange("p h (c t) -> p (h c) t", t=GC)
            V.tensor_tensor(seg[:, :, :].rearrange("p h (c t) -> p (h c) t", t=GC),
                            c4[:, :, GC - 1:GC].broadcast_to([P, GH * NC_, GC]), c4, ALU.subtract).then_inc(g["tmc"], 1)
            mods(6)
            dve.wait_ge(g["ep"], 1)
            V.tensor_tensor(xproj[:, GQ:GQ + 4, :], xproj[:, GQ:GQ + 4, :], ep[:, :, :], ALU.mult)
            dve.wait_ge(g["te"], 1)
            link(V.tensor_tensor(ke[:, :, :], xproj[:, GK:GK + 4, :], seg[:, :, :], ALU.mult))
            dve.wait_ge(g["en"], 1)
            link(V.tensor_tensor(xproj[:, GK:GK + 4, :], xproj[:, GK:GK + 4, :], en[:, :, :], ALU.mult))

            def chunks(t, a):
                return t.rearrange("p h (c t) -> p h c t", t=GC)[:, :, a::2, :]
            kd = xproj[:, GK:GK + 4, :]
            V.tensor_copy(chunks(m13[:, :, :], 0), chunks(ke[:, :, :], 0))
            V.tensor_copy(chunks(m13[:, :, :], 1), chunks(kd, 1))
            V.tensor_tensor(u2[:, :, 0:GC], ke[:, :, 0:GC], et[:, :, 1:2].broadcast_to([P, GH, GC]), ALU.mult)
            link(V.tensor_copy(u2[:, :, GC:P], ke[:, :, GC:P]))
            V.tensor_tensor(u4[:, :, :], u2[:, :, :], et[:, :, 2:3].broadcast_to([P, GH, P]), ALU.mult)\
                .then_inc(g["keys"], 1)
            mods(7)
            dve.wait_ge(g["rexp"], 1)
            link(V.tensor_scalar(sil[:, :, :], sil[:, :, :], 1.0, None, ALU.add))
            link(V.reciprocal(sil[:, :, :], sil[:, :, :]))
            link(V.tensor_tensor(xproj[:, GR:GR + 8, :], xproj[:, GR:GR + 8, :], sil[:, :, :], ALU.mult))
            dve.wait_ge(g["std"], 1)
            link(V.reciprocal(gstd[:, :, :], gstd[:, :, :]))
            dve.wait_ge(g["o"], 4)
            for v in range(2):
                ov = xproj[:, GV + v:GV + 8:2, :]
                ins = V.scalar_tensor_tensor(ov, ov, vecs[:, V_GLAG + v:V_GLAG + v + 1], gstd[:, :, :], ALU.mult, ALU.mult)
            link(ins)
            V.tensor_tensor(xproj[:, GR:GR + 8, :], xproj[:, GR:GR + 8, :], xproj[:, GV:GV + 8, :], ALU.mult)\
                .then_inc(g["res"], 1)
            for k in range(2):
                dve.wait_ge(g["hh"], k + 1)
                V.tensor_tensor(hid_hl[:, 4 * k:4 * k + 4, 1, :], xproj[:, GR + 4 * k:GR + 4 * k + 4, :],
                                hid_hl[:, 4 * k:4 * k + 4, 0, :].bitcast(F32), ALU.subtract).then_inc(mix_ready, 1)
            mods(8)
            dve.wait_ge(n_["std"], 1)
            link(V.reciprocal(nt[:, :, :], nt[:, :, :]))
            for lo, blk, n, vcol in ((0, NQ, 8, V_QG), (8, SK, 2, V_KG), (10, WK, 2, V_KG)):
                xb = xproj[:, blk:blk + n, :]
                ins = V.scalar_tensor_tensor(xb, xb, vecs[:, vcol:vcol + 1], nt[:, lo:lo + n, :], ALU.mult, ALU.mult)
                if lo:
                    ins.then_inc(n_["normed"], 1)
            dve.wait_ge(n_["normed"], 2)
            for dst, blk, vcol in ((kcpk, CK, V_POSK), (kcpv, CV, V_POSV)):
                for b in range(2):
                    for a in range(2):
                        src = xproj[:, blk + b, 16 * a:16 * a + 240].rearrange("p (n r) -> p r n", r=16)
                        pos = vecs[:, vcol + 16 * a:vcol + 16 * a + 16].unsqueeze(2).broadcast_to([P, 16, NCMP])
                        ins = V.tensor_tensor(dst[:, 16 * a:16 * a + 16, b, :], src, pos, ALU.add)
            ins.then_inc(n_["kcp"], 1)
            mods(9)
            dve.wait_ge(n_["hexp"], 1)
            link(V.tensor_scalar(he[:, :, 0:30], he[:, :, 0:30], 1.0, None, ALU.add))
            link(V.reciprocal(he[:, :, 0:30], he[:, :, 0:30]))
            V.tensor_tensor(hk[:, :, 0:30], hk[:, :, 0:30], he[:, :, 0:30], ALU.mult).then_inc(n_["hid"], 1)
            dve.wait_ge(n_["gexp"], 1)
            link(V.tensor_scalar(gt[:, :, :], gt[:, :, :], 1.0, None, ALU.add))
            link(V.reciprocal(gt[:, :, :], gt[:, :, :]))
            dve.wait_ge(n_["kcstd"], 1)
            link(V.reciprocal(kcs[:, 0:30], kcs[:, 0:30]))
            V.scalar_tensor_tensor(kcn[:, 0:30], kcn[:, 0:30], vecs[:, V_KG:V_KG + 1], kcs[:, 0:30], ALU.mult, ALU.mult)\
                .then_inc(n_["kcn"], 1)
            mods(10)
            dve.wait_ge(n_["cl_mm"], 1)
            lc = PS[:, 2:4, 0:240].rearrange("p g (a h n) -> p g a h n", a=TT, n=NCMP)

            def over_heads(m):
                return m.unsqueeze(2).broadcast_to([P, TT, NH, NCMP])

            def over_blocks(m):
                return m.unsqueeze(3).broadcast_to([P, TT, NH, NCMP])
            for a in range(TT):
                for gp in range(2):
                    ins = V.tensor_tensor(sc[:, a, gp::2, :], lc[:, gp, a],
                                          cmask[:, 0, a].unsqueeze(1).broadcast_to([P, NH // 2, NCMP]), ALU.add)
            link(ins)
            link(V.tensor_reduce(cst[:, 0], sc[:, :, :, :], AX.X, ALU.max))
            V.tensor_tensor(sc[:, :, :, :], sc[:, :, :, :], over_blocks(cst[:, 0]), ALU.subtract).then_inc(n_["csub"], 1)
            dve.wait_ge(n_["cexp"], 1)
            link(V.tensor_reduce(cst[:, 1], sc[:, :, :, :], AX.X, ALU.add))
            link(V.reciprocal(cst[:, 1], cst[:, 1]))
            gview = gt[:, :, :].rearrange("p a (h b) -> p a h b", b=3)
            link(V.tensor_tensor(cst[:, 1], cst[:, 1], gview[:, :, :, 0], ALU.mult))
            for a in range(TT):
                ins = V.tensor_tensor(sc[:, a], sc[:, a], cmask[:, 1, a].unsqueeze(1).broadcast_to([P, NH, NCMP]), ALU.mult)
            link(ins)
            V.tensor_tensor(sc[:, :, :, :], sc[:, :, :, :], over_blocks(cst[:, 1]), ALU.mult).then_inc(n_["pc"], 1)
            mods(11)
            def pair_out(k):
                dve.wait_ge(n_["o_mm"], 2 * k + 2)
                V.tensor_copy(nso[:, k, :], PS[:, 6 + k % 2, 0:T]).then_inc(n_["o"], 1)

            dve.wait_ge(n_["kdup_in"], 128)
            for h in range(NH):
                b = h % 2
                dve.wait_ge(n_["l_mm"], h + 1)
                if h >= 2:
                    dve.wait_ge(n_["t_mm"], h - 1)
                lb = PS[:, 2 * b:2 * b + 2, 0:384]
                mk = amask[:, :, :].rearrange("p b t -> p (b t)").unsqueeze(1).broadcast_to([P, 2, 384])
                link(V.tensor_tensor(pb[:, b], lb, mk, ALU.add))
                V.tensor_reduce(hst[:, b, 0, :, 0], pb[:, b, :, 0:P], AX.X, ALU.max)
                link(V.tensor_reduce(hst[:, b, 0, :, 1], pb[:, b, :, P:384], AX.X, ALU.max))
                V.tensor_scalar(hst[:, b, 1], hst[:, b, 0], -DH ** -0.5, None, ALU.mult).then_inc(n_["mx"], 1)
                dve.wait_ge(n_["exp"], h + 1)
                link(V.reciprocal(hst[:, b, 3], hst[:, b, 2]))
                link(V.tensor_tensor(hst[:, b, 3], hst[:, b, 3], gview[:, :, h, 1:3].rearrange("p a b -> p b a"), ALU.mult))
                for br in range(2):
                    for tt, (lo, hi) in enumerate(((0, P), (P, 384))):
                        ins = V.tensor_scalar(pb[:, b, br, lo:hi], pb[:, b, br, lo:hi], hst[:, b, 3, br, tt:tt + 1], None,
                                              ALU.mult)
                ins.then_inc(n_["pn"], 1)
                if h % 2 == 0 and h >= 2:
                    pair_out(h // 2 - 1)
            pair_out(NH // 2 - 1)
            for k in range(2):
                dve.wait_ge(n_["hh"], k + 1)
                V.tensor_tensor(hid_hl[:, 8 + 4 * k:12 + 4 * k, 1, :], nso[:, 4 * k:4 * k + 4, :],
                                hid_hl[:, 8 + 4 * k:12 + 4 * k, 0, :].bitcast(F32), ALU.subtract).then_inc(mix_ready, 1)

            for a in range(4):
                pieces = []
                if a in (1, 2):
                    pieces = sum((mod_pieces(j, (30 + 4 * j, 15 + 2 * j)) for j in (12 + 2 * (a - 1), 13 + 2 * (a - 1))), [])
                segment(P_OUT0 + a, pieces)
                p = P_OUT0 + a
                evac_add(p, p // 2, p % 2, a)
            if upto < 2:
                return

            def mlp(l, p0, last, mods_):
                def quarter(q, final=False):
                    for a in range(8):
                        n = 16 * l + 4 * q + a

                        def before(k, a=a, n=n):
                            if not 1 <= a <= 4:
                                return
                            if k == 1:
                                dve.wait_ge(psum_free[(p0 + a - 1) % 2], (p0 + a - 1) // 2 + 4 * q + 2)
                                V.tensor_tensor(relu[:, :, :], relu[:, :, :], relu[:, :, :], ALU.mult)\
                                    .then_inc(sq_done, 1)
                            if k == 4:
                                dve.wait_ge(hidh_done, n)
                                V.tensor_tensor(hid_hl[:, 4 * (a - 1):4 * a, 1, :], relu[:, :, :],
                                                hid_hl[:, 4 * (a - 1):4 * a, 0, :].bitcast(F32), ALU.subtract)\
                                    .then_inc(hid_ready, 1)
                        pieces = []
                        if mods_ and a % 2 == 0:
                            j = 4 * q + a // 2
                            pieces = mod_pieces(j, (94 + 4 * j, 47 + 2 * j))
                        p = p0 + 8 * q + a
                        if final and a == 7:
                            for h in range(4, 8):
                                half(p, h)
                        else:
                            segment(p, pieces, before)
                        if a >= 4:
                            evac_add(p, (p0 + a) // 2 + 4 * q, (p0 + a) % 2, a - 4)
                with dve.Fori(0, 3 if last else 4) as q:
                    quarter(q)
                if last:
                    quarter(3, True)

            fold(1, 3, 0, 3 * KC, V_BMLP, V_NMLP, (9, 9))
            norm(1)
            dve.wait_ge(acc_clear, 2)
            mlp(0, P_MLP0, False, True)
            if upto < 3:
                return
            fold(2, 4, 0, 3 * KC, V_BMIX + 48, V_NMIX + 16, (25, 25))
            norm(2)
            dve.wait_ge(acc_clear, 5)

            def mods1(j):
                return mod_pieces(j, (158 + 4 * j, 79 + 2 * j))
            with dve.Fori(0, 5) as i:
                for a in range(2):
                    segment(P_PROJ1 + 2 * i + a, mods1(2 * i + a))
            segment(P_PROJ1 + 10, mods1(10))
            segment(P_PROJ1 + 11, mods1(11), cols2=P)
            segment(P_PROJ1 + 12, cols=P)
            dve.wait_ge(psum_free[0], P_PROJ1 // 2 + 7 + 1)
            dve.wait_ge(psum_free[1], P_PROJ1 // 2 + 6 + 1)
            for k in range(4):
                if k:
                    dve.wait_ge(m_["cv"], k)
                for tap in range(3, -1, -1):
                    d = 3 - tap
                    for b in range(4):
                        m = 4 * k + b
                        wcol = vecs[:, V_CONV + 16 * tap + m:V_CONV + 16 * tap + m + 1]
                        if d == 0:
                            ins = V.tensor_scalar(cva[:, b, :], xproj[:, m, :], wcol, None, ALU.mult)
                        else:
                            ins = V.scalar_tensor_tensor(cva[:, b, d:T], xproj[:, m, 0:T - d], wcol, cva[:, b, d:T],
                                                         ALU.mult, ALU.add)
                    link(ins)
                V.tensor_copy(xproj[:, 4 * k:4 * k + 4, :], cva[:, :, :]).then_inc(m_["cv"], 1)
                if k % 2 == 1:
                    e = k // 2
                    dve.wait_ge(m_["cexp"], e + 1)
                    link(V.tensor_scalar(cvs[:, :, :], cvs[:, :, :], 1.0, None, ALU.add))
                    link(V.reciprocal(cvs[:, :, :], cvs[:, :, :]))
                    V.tensor_tensor(xproj[:, 8 * e:8 * e + 8, :], xproj[:, 8 * e:8 * e + 8, :], cvs[:, :, :], ALU.mult)\
                        .then_inc(m_["silu"], 1)
            for piece in mods1(12):
                piece()
            dve.wait_ge(m_["gcopy"], 1)
            V.scalar_tensor_tensor(mg[:, 1, :, 4:8], mg[:, 0, :, 4:8], -1.0, mg[:, 0, :, 4:8], ALU.mult, ALU.min)\
                .then_inc(m_["gabs"], 1)
            dve.wait_ge(m_["gln"], 1)
            V.scalar_tensor_tensor(mg[:, 0, :, 4:8], mg[:, 0, :, 4:8], 0.0, mg[:, 2, :, 4:8], ALU.min, ALU.subtract)\
                .then_inc(m_["lf"], 1)
            for piece in mods1(13):
                piece()
            dve.wait_ge(m_["b_mm"], 1)
            link(V.tensor_copy(brows[0:4, 0, :], PS[0:4, 5, 0:T]))
            link(V.tensor_tensor(brows[0:4, 1, :], PS[0:4, 5, T:2 * T], brows[0:4, 0, :], ALU.subtract))
            link(V.tensor_tensor_scan(brows[0:4, 2, :], brows[0:4, 1, :], brows[0:4, 1, :], 0.0, ALU.max, ALU.max))
            V.tensor_tensor(brows[0:4, 0, :], brows[0:4, 0, :], brows[0:4, 2, :], ALU.add).then_inc(m_["rows"], 1)
            for piece in mods1(14):
                piece()
            dve.wait_ge(acc_clear, 4)
            V.tensor_copy(selh[0:4, :], ident[0:4, 0:1].broadcast_to([4, P])).then_inc(m_["sel"], 1)
            mrow = amask[:, :, :].rearrange("p b t -> p (b t)")
            for h in range(MH):
                b = h % 2
                dve.wait_ge(m_["bc_mm"], h + 1)
                if h >= 2:
                    dve.wait_ge(m_["sd"], h - 1)
                V.scalar_tensor_tensor(dm[:, b, 0:256], PS[:, 5, 0:T], -1.0, mrow[:, 0:256], ALU.mult, ALU.add)
                V.scalar_tensor_tensor(dm[:, b, 256:384], PS[:, 5, P:T], -1.0, mrow[:, 256:384], ALU.mult, ALU.add)\
                    .then_inc(m_["dpre"], 1)
                if h + 1 < MH:
                    V.tensor_copy(selh[0:4, :], ident[0:4, h + 1:h + 2].broadcast_to([4, P])).then_inc(m_["sel"], 1)
                dve.wait_ge(m_["s_mm"], h + 1)
                dve.wait_ge(m_["d"], h + 1)
                V.scalar_tensor_tensor(sd[:, b, :], PS[:, 4, 0:384], MDK ** -0.5, dm[:, b, :], ALU.mult, ALU.mult)\
                    .then_inc(m_["sd"], 1)
                dve.wait_ge(m_["em"], h + 1)
                dve.wait_ge(m_["num_mm"], h + 1)
                if h >= 1:
                    dve.wait_ge(m_["h"], h)
                link(V.tensor_scalar(mden[:, :], PS[:, 6, 0:T], -1.0, None, ALU.mult))
                link(V.tensor_tensor(mden[:, :], PS[:, 6, 0:T], mden[:, :], ALU.max))
                link(V.tensor_tensor(mden[:, :], mden[:, :], mexp[:, :], ALU.max))
                link(V.reciprocal(mden[:, :], mden[:, :]))
                hb = xproj[:, MV + 4 * h:MV + 4 * h + 4, :]
                V.tensor_tensor(hb, PS[:, 2 * b:2 * b + 2, :].rearrange("p k (b t) -> p (k b) t", t=T),
                                mden[:, :].unsqueeze(1).broadcast_to([P, 4, T]), ALU.mult).then_inc(m_["h"], 1)
                dve.wait_ge(m_["std"], h + 1)
                link(V.reciprocal(std[:, :], std[:, :]))
                for v in range(4):
                    ins = V.scalar_tensor_tensor(hb[:, v, :], hb[:, v, :], vecs[:, V_MLG + v:V_MLG + v + 1], std[:, :],
                                                 ALU.mult, ALU.mult)
                link(ins)
                dve.wait_ge(m_["oexp"], h + 1)
                link(V.tensor_scalar(msq[:, :, :], msq[:, :, :], 1.0, None, ALU.add))
                link(V.reciprocal(msq[:, :, :], msq[:, :, :]))
                V.tensor_tensor(xproj[:, MO + 4 * h:MO + 4 * h + 4, :], hb, msq[:, :, :], ALU.mult)\
                    .then_inc(m_["res"], 1)
                if h == 0:
                    for piece in mods1(15):
                        piece()
            for h in range(MH):
                dve.wait_ge(m_["hh"], h + 1)
                V.tensor_tensor(hid_hl[:, 4 * h:4 * h + 4, 1, :], xproj[:, MO + 4 * h:MO + 4 * h + 4, :],
                                hid_hl[:, 4 * h:4 * h + 4, 0, :].bitcast(F32), ALU.subtract).then_inc(mix_ready, 1)
            for a in range(4):
                segment(P_OUT1 + a)
                p = P_OUT1 + a
                evac_add(p, p // 2, p % 2, a)
            if upto < 4:
                return
            fold(3, 5, 0, 3 * KC, V_BMLP + 48, V_NMLP + 16, (34, 33))
            norm(3)
            mlp(1, P_MLP1, True, False)

        @block.tensor
        def _(pe):
            mm = nc.tensor.matmul
            pe.sem_inc(half_done, 4)
            pe.sem_inc(psum_free[0], 1)
            pe.sem_inc(psum_free[1], 1)

            def panel(p, ph, par, src, ready=None, nb=4):
                pe.wait_ge(psum_free[par], ph + 1)
                for h in range(8):
                    if ready and h % 2 == 0:
                        ready(h // 2)
                    pe.wait_ge(wl_ready, 8 * p + h + 9)
                    for kk in range(2):
                        kc = 2 * h + kk
                        for b in range(nb):
                            o_ = PS[:, 2 * par + b // 2, T * (b % 2):T * (b % 2) + T]
                            w_h, w_l = wh[:, h % 4, kk, P * b:P * b + P], wl[:, h % 4, kk, P * b:P * b + P]
                            mm(o_, w_h, src[:, kc, 0, :], start=(kc == 0 and b % 2 == 0), stop=False,
                               skip_group_check=True)
                            mm(o_, w_h, src[:, kc, 1, :], start=False, stop=False, skip_group_check=True)
                            ins = mm(o_, w_l, src[:, kc, 0, :], start=False, stop=(kc == KC - 1),
                                     skip_group_check=True)
                    ins.then_inc(half_done, 1)

            def fold(lo, hi, sem_, value):
                pe.wait_ge(sem_, value)
                for m in range(lo, hi):
                    ins = mm(PS[:, 6, m:m + 1], acc[:, P * m:P * m + P], ones[:, 0:1], start=True, stop=True)
                ins.then_inc(fold_done, 1)

            def norm(n):
                for k in range(4):
                    pe.wait_ge(nsq_done, 4 * n + k + 1)
                    for b in range(4):
                        ins = mm(PS[:, 5, 0:T], ones[:, :], sqb[:, k % 2, b, :], start=(k + b == 0),
                                 stop=(k == 3 and b == 3))
                    ins.then_inc(nstat_mm, 1)

            def act_in(n):
                return lambda s: pe.wait_ge(act_ready, 4 * n + s + 1)

            def result():
                pe.wait_ge(psum_free[0], done[0])
                pe.wait_ge(psum_free[1], done[1])
                for k in range(8):
                    a, m0 = k // 4, 4 * (k % 4)
                    if k >= 4:
                        pe.wait_ge(ot_ready, k - 3)
                    for b in range(4):
                        ins = nc.tensor.transpose(PS[:, k % 4, P * b:P * b + P], xT[:, m0 + b, P * a:P * a + P], ident[:, :])
                    ins.then_inc(ot_mm, 1)

            pe.wait_ge(consts_ready, N_CONSTS)
            pe.wait_ge(params_in, 16 * N_PARAMS)
            for k, n in enumerate((124, 96, 96, 96)):
                ins = nc.tensor.transpose(PS[:, 4, P * k:P * k + n], prow[0:n, k, :], ident[0:n, 0:n])
            ins.then_inc(vecs_mm, 1)
            pe.wait_ge(x_in, 16)
            for k in range(8):
                if k >= 4:
                    pe.wait_ge(xt_ready, k - 3)
                for b in range(2):
                    for a in range(2):
                        m = 2 * k + b
                        ins = nc.tensor.transpose(PS[:, k % 4, T * b + P * a:T * b + P * a + P],
                                                  xtok[:, a, P * m:P * m + P], ident[:, :])
                ins.then_inc(xt_mm, 1)
            norm(0)
            fold(0, 2 * KC, start_used, 4 + 33)
            with pe.Fori(0, 3) as i:
                for a in range(2):
                    panel(2 * i + a, i, a, act_hl, act_in(0))
            fold(2 * KC, 3 * KC, mod_used, 2 + 30)
            with pe.Fori(3, 5) as i:
                for a in range(2):
                    panel(2 * i + a, i, a, act_hl, act_in(0))
            panel(10, 5, 0, act_hl, act_in(0))
            panel(11, 5, 1, act_hl, act_in(0), 2)
            if upto < 1:
                return result()
            pe.wait_ge(psum_free[0], 7)
            pe.wait_ge(psum_free[1], 7)
            pe.wait_ge(g["wg_in"], 16)
            for h in range(GH):
                ins = mm(PS[:, 4 + h // 2, T * (h % 2):T * (h % 2) + T], wgate[0:16, GDK * h:GDK * h + GDK],
                         xproj[0:16, ZT, :], start=True, stop=True)
            ins.then_inc(g["gate_mm"], 1)
            for k in range(4):
                for b in range(4):
                    blk = GV + 4 * (k % 2) + b
                    ins = nc.tensor.transpose(PS[:, k, P * b:P * b + P], xproj[:, blk, P * (k // 2):P * (k // 2) + P],
                                              ident[:, :])
                ins.then_inc(g["vt_mm"], 1)
            pe.wait_ge(g["keys"], 1)
            for h in range(GH):
                q = xproj[:, GQ + h, :]
                kdh = xproj[:, GK + h, :]
                for lo, keys, t0 in ((0, kdh[:, 0:P], 0), (GC, m13[:, h, 0:P], 1), (2 * GC, u2[:, h, :], 2),
                                     (3 * GC, u4[:, h, :], 3), (4 * GC, kdh[:, P:T], 2), (5 * GC, m13[:, h, P:T], 3)):
                    ins = mm(PS[:, 4 + h, lo:lo + GC], keys, q[:, GC * t0:GC * t0 + GC], start=True, stop=True)
                ins.then_inc(g["att_mm"], 1)
            pe.wait_ge(g["vt"], 4)
            for h in range(GH):
                pe.wait_ge(g["masked"], h + 1)
                for v in range(2):
                    col = GDV * h + P * v
                    mm(PS[:, h, T * v:T * v + T], vt[:, 0, col:col + P], att[:, h, 0:T], start=True, stop=False)
                    ins = mm(PS[:, h, T * v + P:T * v + T], vt[:, 1, col:col + P], att[:, h, T:384], start=False,
                             stop=True)
                ins.then_inc(g["o_mm"], 1)
            pe.wait_ge(g["att"], 4)
            for h in range(GH):
                pe.wait_ge(g["osq"], h + 1)
                for v in range(2):
                    ins = mm(PS[:, 4 + h // 2, T * (h % 2):T * (h % 2) + T], ones[:, :], gsq[:, h % 2, v, :],
                             start=(v == 0), stop=(v == 1))
                ins.then_inc(g["st_mm"], 1)
            pe.wait_ge(g["o"], 4)
            pe.wait_ge(g["std"], 1)
            pe.wait_ge(n_["sq"], 1)
            for k in range(12):
                ins = mm(PS[:, k // 2, T * (k % 2):T * (k % 2) + T], pair_ones[:, :], nt[:, k, :], start=True, stop=True)
            ins.then_inc(n_["sq_mm"], 1)
            for k in range(2):
                for b, blk in enumerate((SV, SV + 1, WV, WV + 1)):
                    ins = nc.tensor.transpose(PS[:, 6 + k, P * b:P * b + P], xproj[:, blk, P * k:P * k + P], ident[:, :])
            ins.then_inc(n_["vsw_mm"], 1)
            pe.wait_ge(n_["std"], 1)
            for k in range(2):
                ins = nc.tensor.transpose(PS[:, 2, P * k:P * k + P], xproj[:, GT, P * k:P * k + P], ident[:, :])
            ins.then_inc(n_["gt_mm"], 1)
            pe.wait_ge(n_["w1_in"], 64)
            pe.wait_ge(n_["kcp"], 1)
            for kv, (w, src) in enumerate(((w1k, kcpk), (w1v, kcpv))):
                for l in range(32):
                    for gp in range(2):
                        r = slice(DH * gp, DH * gp + DH)
                        ins = mm(PS[r, 4 + kv, 0:30], w[r, l, :], src[r, l, :, :], start=(l == 0), stop=(l == 31))
            ins.then_inc(n_["h_mm"], 1)
            pe.wait_ge(n_["hid"], 1)
            for gp in range(2):
                r = slice(DH * gp, DH * gp + DH)
                mm(PS[r, 4, 64:94], w2k[r, :], hk[r, 0, 0:30], start=True, stop=True)
            for gp in range(2):
                r = slice(DH * gp, DH * gp + DH)
                for b in range(2):
                    ins = mm(PS[0:NCMP, gp, DH * b:DH * b + DH], hk[r, 1, NCMP * b:NCMP * b + NCMP], w2v[r, :],
                             start=True, stop=True)
            ins.then_inc(n_["kc_mm"], 1)
            pe.wait_ge(n_["kcsq"], 1)
            mm(PS[:, 5, 128:158], pair_ones[:, :], kcs[:, 0:30], start=True, stop=True).then_inc(n_["kcsq_mm"], 1)
            pe.wait_ge(n_["kcd_in"], 64)
            pe.wait_ge(n_["normed"], 2)
            pe.wait_ge(n_["gexp"], 1)
            for a in range(TT):
                for h in range(NH):
                    r = slice(DH * (h % 2), DH * (h % 2) + DH)
                    col = NCMP * (NH // 2 * a + h // 2)
                    ins = mm(PS[:, 2 + h % 2, col:col + NCMP], xproj[r, NQ + h // 2, P * a:P * a + P], kcd[r, h // 4, :],
                             start=True, stop=True)
            ins.then_inc(n_["cl_mm"], 1)

            def logits(h):
                b = h % 2
                r = slice(DH * b, DH * b + DH)
                if h >= 2:
                    pe.wait_ge(n_["mx"], h - 1)
                for br in range(2):
                    mm(PS[:, 2 * b + br, 0:P], xproj[r, NQ + h // 2, 0:P], kdup[r, br, h // 4, 0:P], start=True,
                       stop=True)
                    ins = mm(PS[:, 2 * b + br, P:384], xproj[r, NQ + h // 2, P:T], kdup[r, br, h // 4, :], start=True,
                             stop=True)
                ins.then_inc(n_["l_mm"], 1)

            def turned(h):
                b = h % 2
                pe.wait_ge(n_["pn"], h + 1)
                if h >= 1:
                    pe.wait_ge(n_["pt"], h)
                for br in range(2):
                    for k in range(3):
                        nc.tensor.transpose(PS[:, 4 + br, P * k:P * k + P], pb[:, b, br, (0, P, 2 * P)[k]:(P, 2 * P, 3 * P)[k]],
                                            ident[:, :])
                for a in range(TT):
                    ins = mm(PS[0:NCMP, 4 + a, 384:512], sc[:, a, h, :], ident[:, :], start=True, stop=True)
                ins.then_inc(n_["t_mm"], 1)

            def values(h):
                b = h % 2
                r = slice(DH * b, DH * b + DH)
                gcol = DH * (h // 4)
                pe.wait_ge(n_["pt"], h + 1)
                if b == 0 and h >= 4:
                    pe.wait_ge(n_["o"], h // 2 - 1)
                o_ = PS[r, 6 + (h // 2) % 2, 0:T]
                for br in range(2):
                    v0, v1 = vsw[:, 0, br, gcol:gcol + DH], vsw[:, 1, br, gcol:gcol + DH]
                    mm(o_, v0, pt[:, b, br, 0:T], start=(br == 0), stop=False, skip_group_check=True)
                    mm(o_[:, P:T], v1, pt[:, b, br, T:384], start=False, stop=False, skip_group_check=True)
                ins = mm(o_, vcm[0:NCMP, gcol:gcol + DH], ptc[0:NCMP, b, :], start=False, stop=True,
                         skip_group_check=True)
                ins.then_inc(n_["o_mm"], 1)

            pe.wait_ge(n_["vc"], 1)
            pe.wait_ge(n_["kdup_in"], 128)
            logits(0)
            pe.wait_ge(n_["pc"], 1)
            pe.wait_ge(n_["vsw"], 2)
            for h in range(NH):
                if h + 1 < NH:
                    logits(h + 1)
                if h >= 1:
                    values(h - 1)
                turned(h)
            values(NH - 1)

            def mix_in(l):
                return lambda s: pe.wait_ge(mix_ready, 4 * l + s + 1)
            with pe.Fori(0, 2) as i:
                for a in range(2):
                    panel(P_OUT0 + 2 * i + a, P_OUT0 // 2 + i, a, hid_hl, mix_in(0))
            if upto < 2:
                return result()

            def mlp(l, p0):
                with pe.Fori(0, 4) as q:
                    with pe.Fori(0, 2) as i:
                        for a in range(2):
                            par = (p0 + a) % 2
                            panel(p0 + 8 * q + 2 * i + a, (p0 + a) // 2 + 4 * q + i, par, act_hl, act_in(2 * l + 1))
                    with pe.Fori(0, 2) as i:
                        for a in range(2):
                            par = (p0 + a) % 2
                            panel(p0 + 4 + 8 * q + 2 * i + a, (p0 + 4 + a) // 2 + 4 * q + i, par, hid_hl,
                                  lambda s: pe.wait_ge(hid_ready, 16 * l + 4 * q + s + 2))
            fold(0, 3 * KC, mod_used, 2 + 94)
            norm(1)
            mlp(0, P_MLP0)
            if upto < 3:
                return result()
            fold(0, 3 * KC, mod_used, 2 + 158)
            norm(2)
            with pe.Fori(0, 6) as i:
                for a in range(2):
                    panel(P_PROJ1 + 2 * i + a, P_PROJ1 // 2 + i, a, act_hl, act_in(2))
            panel(P_PROJ1 + 12, P_PROJ1 // 2 + 6, 0, act_hl, act_in(2), 1)
            pe.wait_ge(psum_free[0], P_PROJ1 // 2 + 7 + 1)
            pe.wait_ge(psum_free[1], P_PROJ1 // 2 + 6 + 1)
            for a in range(TT):
                mm(PS[:, 4, P * a + 120:P * a + 128], gates[:, P * a:P * a + P], ident[:, 120:128], start=True,
                   stop=False, skip_group_check=True)
                ins = mm(PS[:, 4, P * a + 120:P * a + 128], ones[0:1, :], brow[0:1, :], start=False, stop=True,
                         skip_group_check=True)
            ins.then_inc(m_["gt_mm"], 1)
            pe.wait_ge(m_["silu"], 2)
            for k in range(8):
                if k >= 4:
                    pe.wait_ge(m_["vt"], k - 3)
                for b in range(4):
                    blk = MV + 4 * (k % 4) + b
                    ins = nc.tensor.transpose(PS[:, k % 4, P * b:P * b + P], xproj[:, blk, P * (k // 4):P * (k // 4) + P],
                                              ident[:, :])
                ins.then_inc(m_["vt_mm"], 1)
            pe.wait_ge(m_["lf"], 1)
            mm(PS[0:4, 5, 0:T], mg[:, 0, 0, 4:8], upper[:, :, :].rearrange("p a t -> p (a t)"), start=True, stop=False,
               skip_group_check=True)
            mm(PS[0:4, 5, P:T], mg[:, 0, 1, 4:8], upper[:, 0, :], start=False, stop=True, skip_group_check=True)
            for a in range(TT):
                ins = mm(PS[0:4, 5, T + P * a:T + P * a + P], mg[:, 0, a, 0:4], ident[:, :], start=True, stop=True)
            ins.then_inc(m_["b_mm"], 1)
            pe.wait_ge(m_["rows"], 1)
            for a in range(TT):
                ins = mm(PS[:, 6, 8 * a:8 * a + 4], brows[0:4, 1, P * a:P * a + P], ident[0:4, 0:4], start=True, stop=True)
            ins.then_inc(m_["a_mm"], 1)
            pe.wait_ge(m_["gcopy"], 1)
            pe.wait_ge(m_["acol"], 1)
            pe.wait_ge(m_["vt"], 8)
            for h in range(MH):
                b = h % 2
                if h >= 1:
                    pe.wait_ge(m_["dpre"], h)
                    pe.wait_ge(m_["em"], h)
                pe.wait_ge(m_["sel"], h + 1)
                mm(PS[:, 5, 0:T], selh[0:4, :], brows[0:4, 2, :], start=True, stop=True)
                mm(PS[:, 5, T:2 * T], selh[0:4, :], brows[0:4, 0, :], start=True, stop=True).then_inc(m_["bc_mm"], 1)
                if h >= 1:
                    pe.wait_ge(m_["sd"], h)
                for kc in range(2):
                    qh, kh = xproj[:, MQ + 2 * h + kc, :], xproj[:, MK + 2 * h + kc, :]
                    mm(PS[:, 4, 0:T], kh[:, 0:P], qh, start=(kc == 0), stop=False, skip_group_check=True)
                    ins = mm(PS[:, 4, T:384], kh[:, P:T], qh[:, P:T], start=False, stop=(kc == 1), skip_group_check=True)
                ins.then_inc(m_["s_mm"], 1)
                pe.wait_ge(m_["sd"], h + 1)
                if h >= 1:
                    pe.wait_ge(m_["h"], h)
                mm(PS[:, 6, 0:T], ones[:, :], sd[:, b, 0:T], start=True, stop=False)
                mm(PS[:, 6, P:T], ones[:, :], sd[:, b, T:384], start=False, stop=True)
                for v in range(4):
                    col = MDV * h + P * v
                    bank, t0 = 2 * b + v // 2, T * (v % 2)
                    mm(PS[:, bank, t0:t0 + T], mvt[:, 0, col:col + P], sd[:, b, 0:T], start=True, stop=False)
                    ins = mm(PS[:, bank, t0 + P:t0 + T], mvt[:, 1, col:col + P], sd[:, b, T:384], start=False, stop=True)
                ins.then_inc(m_["num_mm"], 1)
                pe.wait_ge(m_["hsq"], h + 1)
                for v in range(4):
                    ins = mm(PS[:, 7, 0:T], ones[:, :], msq[:, v, :], start=(v == 0), stop=(v == 3))
                ins.then_inc(m_["st_mm"], 1)
            for a in range(4):
                p = P_OUT1 + a
                panel(p, p // 2, p % 2, hid_hl, mix_in(1))
            if upto < 4:
                return result()
            fold(0, 3 * KC, mod_used, 2 + 222)
            norm(3)
            mlp(1, P_MLP1)
            result()


_INS = ['x', 'c', 'norm_mix_g', 'mod_mix_w', 'mod_mix_b', 'norm_mlp_g', 'mod_mlp_w', 'mod_mlp_b', 'mlp_w1', 'mlp_w2',
        'ab_w_in', 'ab_w_out', 'gla_w_gate', 'gla_b_gate', 'gla_norm_g', 'nsa_q_norm_g', 'nsa_k_norm_g',
        'nsa_cmp_pos_k', 'nsa_cmp_pos_v', 'nsa_cmp_k_w1', 'nsa_cmp_k_w2', 'nsa_cmp_v_w1', 'nsa_cmp_v_w2', 'ml_w_in',
        'ml_w_out', 'ml_conv_w', 'ml_b_i', 'ml_b_f', 'ml_norm_g']
UPTO = 99


def kernel(**inputs):
    import numpy as _np
    import concourse.bacc as _bacc
    from concourse import mybir as _mybir
    from concourse.bass_utils import run_bass_kernel_spmd as _run

    nc = _bacc.Bacc("TRN2", target_bir_lowering=False, num_devices=1)
    arrays, args = {}, []
    for name in _INS:
        a = _np.ascontiguousarray(inputs[name])
        arrays[f"in_{name}_dram"] = a
        args.append(nc.dram_tensor(f"in_{name}_dram", a.shape, _mybir.dt.from_np(a.dtype), kind="ExternalInput").ap())
    out = nc.dram_tensor("out_dram", (1, T, D), F32, kind="ExternalOutput").ap()
    trunk(nc, *args, out, upto=UPTO)
    r = _run(nc, [arrays], core_ids=[0])
    return r.results[0]["out_dram"]
```

```python
import concourse.bass as bass
from concourse import mybir
from contextlib import ExitStack

F32 = mybir.dt.float32
F32R = mybir.dt.float32r
ALU = mybir.AluOpType
ACT = mybir.ActivationFunctionType
AX = mybir.AxisListType

P = 128
D = 2048
T = 256
KC = D // P
TT = T // P
NEG = -1e30
EPS = 1e-6
GH, GDK, GDV, GTAU = 4, 128, 256, 16.0
GC = 64
NC_ = T // GC
NH, NG, DH = 16, 4, 64
NCMP = (T - 32) // 16 + 1
MH, MDK, MDV = 4, 256, 512
GLA_COLS = 2 * GH * GDK + 2 * GH * GDV + 16
AB_COLS = 5696
ML_COLS = 6152

P_PROJ0, P_OUT0, P_MLP0, P_PROJ1, P_OUT1, P_MLP1, P_END = 0, 12, 16, 48, 61, 65, 97

GQ, GK, GV, GR, NQ, CK, CV, SK, SV, WK, WV, ZT, GT = 0, 4, 8, 16, 24, 32, 34, 36, 38, 40, 42, 44, 45
MQ, MK, MV, MO, MG = 0, 8, 16, 32, 48

V_C, V_NMIX, V_NMLP, V_BG, V_GLAG, V_QG, V_KG, V_MLG, V_POSK = 0, 16, 48, 80, 84, 86, 87, 88, 92
V_CONV, V_POSV, V_BMIX, V_BMLP, V_N = 124, 188, 220, 316, 412
N_PARAMS, N_CONSTS = 22, 16


def trunk(nc, x, c, norm_mix_g, mod_mix_w, mod_mix_b, norm_mlp_g, mod_mlp_w, mod_mlp_b, mlp_w1, mlp_w2,
          ab_w_in, ab_w_out, gla_w_gate, gla_b_gate, gla_norm_g, nsa_q_norm_g, nsa_k_norm_g, nsa_cmp_pos_k,
          nsa_cmp_pos_v, nsa_cmp_k_w1, nsa_cmp_k_w2, nsa_cmp_v_w1, nsa_cmp_v_w2, ml_w_in, ml_w_out, ml_conv_w,
          ml_b_i, ml_b_f, ml_norm_g, out):
    ctx = ExitStack()
    with ctx:
        arena = ctx.enter_context(nc.sbuf_tensor("arena", [P, 53200], F32))
        base = 16512

        def at(name, off, shape, dt=F32):
            return nc.alloc_sbuf_tensor_at(name, shape, dt, offset=base + off)

        O_X = 16384
        o_act = O_X
        o_prj = o_act + 32768
        o_raw = o_prj + 49152
        o_wh = o_raw + 32768
        o_wl = o_wh + 16384
        o_mr = o_wl + 16384
        o_acc = o_mr + 12288
        o_small = o_acc + 24576
        xT = at("xT", 0, [P, KC, T])
        act_hl = at("act_hl", o_act, [P, KC, 2, T], F32R)
        hid_hl = at("hid_hl", o_prj, [P, KC, 2, T], F32R)
        xproj = at("xproj", o_prj, [P, 48, T])
        raw = at("raw", o_raw, [P, 4, 4, 512])
        wh = at("wh", o_wh, [P, 4, 2, 512], F32R)
        wl = at("wl", o_wl, [P, 4, 2, 512], F32R)
        modring = at("modring", o_mr, [P, 2, 1536])
        acc = at("acc", o_acc, [P, 3 * D])
        o = o_small
        small = {}
        for name, shape in (("ident", [P, P]), ("ones", [P, P]), ("pair_ones", [P, P]), ("amask", [P, 3, P]),
                            ("cmask", [P, 2, TT, NCMP]), ("upper", [P, 2, P]), ("vecs", [P, V_N]),
                            ("modv", [P, 3, KC]), ("siluc", [P, KC]), ("std", [P, T]), ("gates", [P, T]),
                            ("w2k", [P, DH]), ("w2v", [P, DH]), ("brow", [1, 8]), ("eps", [P, 1])):
            n = 4
            for d in shape[1:]:
                n *= d
            small[name] = at(name, o, shape)
            o += (n + 31) // 32 * 32
        assert base + o <= 229344, base + o - 229344
        ident, ones, pair_ones, amask, cmask = (small[n] for n in ("ident", "ones", "pair_ones", "amask", "cmask"))
        upper, vecs, modv, siluc, std, gates = (small[n] for n in ("upper", "vecs", "modv", "siluc", "std", "gates"))
        w2k, w2v, brow, eps = (small[n] for n in ("w2k", "w2v", "brow", "eps"))
        xtok = at("xtok", o_act, [P, TT, D])
        startring = at("startring", o_prj, [P, 4, D])
        prow = at("prow", o_prj + 32768, [P, 4, P])
        sqb = at("sqb", o_prj + 32768, [P, 2, 4, T])
        xnb = at("xnb", o_prj + 40960, [P, 2, 4, T])
        relu = at("relu", o_prj + 32768, [P, 4, T])
        wgate = at("wgate", o_prj + 46 * 1024, [16, GH * GDK])
        K_ = 1024
        vt = at("vt", o_prj + GV * K_, [P, TT, GH * GDV])
        go = at("go", o_act, [P, 2 * GH, T])
        la = at("la", o_act + 8 * K_, [P, GH, T])
        m13 = at("m13", o_act + 8 * K_, [P, GH, T])
        ep = at("ep", o_act + 12 * K_, [P, GH, T])
        u2 = at("u2", o_act + 12 * K_, [P, GH, P])
        u4 = at("u4", o_act + 14 * K_, [P, GH, P])
        ke = at("ke", o_act + 16 * K_, [P, GH, T])
        cum = at("cum", o_act + 20 * K_, [P, GH, T])
        seg = at("seg", o_act + 24 * K_, [P, GH, T])
        en = at("en", o_act + 28 * K_, [P, GH, T])
        et = at("et", o_prj + 44 * 1024, [P, GH, NC_])
        att = at("att", o_act + 16 * K_, [P, GH, 384])
        gstd = at("gstd", o_act + 22 * K_, [P, GH, T])
        gsq = at("gsq", o_act + 26 * K_, [P, 2, 2, T])
        w1k = at("w1k", o_act + 8 * K_, [P, 32, DH])
        w1v = at("w1v", o_act, [P, 32, DH])
        nt = at("nt", o_act + 16 * K_, [P, 12, T])
        kcpk = at("kcpk", o_act + 16 * K_, [P, 32, 2, NCMP])
        kcpv = at("kcpv", o_act + 20 * K_, [P, 32, 2, NCMP])
        kdup = at("kdup", o_act + 24 * K_, [P, 2, NG, T])
        vsw = at("vsw", o_prj + CK * K_, [P, TT, 2, NG * DH])
        nso = at("nso", o_act, [P, 8, T])
        pb = at("pb", o_act + 8 * K_, [P, 3, 2, 384])
        pt = at("pt", o_act + 17 * K_, [P, 2, 2, 384])
        ptc = at("ptc", o_prj + WK * K_, [16, 2, T])
        sc = at("sc", o_prj + WV * K_, [P, TT, NH, NCMP])
        q_ = o_prj + SV * K_
        hk = at("hk", q_, [P, 2, 32])
        he = at("he", q_ + 256, [P, 2, 32])
        kcn = at("kcn", q_ + 512, [P, 32])
        kcs = at("kcs", q_ + 640, [P, 32])
        kcd = at("kcd", q_ + 768, [P, NG, 2, NCMP])
        gt = at("gt", q_ + 1280, [P, TT, 48])
        cst = at("cst", q_ + 1664, [P, 3, TT, NH])
        vcm = at("vcm", o_prj + (SK) * K_, [16, NG * DH])
        hst = at("hst", o_prj + (SK + 1) * K_, [P, 2, 4, 2, 2])
        mvt = at("mvt", o_prj + MV * K_, [P, TT, D])
        mh = at("mh", o_act, [P, 4 * MH, T])
        dm = at("dm", o_act + 16 * K_, [P, 2, 384])
        sd = at("sd", o_act + 19 * K_, [P, 2, 384])
        mden = at("mden", o_act + 22 * K_, [P, T])
        mexp = at("mexp", o_act + 23 * K_, [P, T])
        msq = at("msq", o_act + 24 * K_, [P, 4, T])
        mg = at("mg", o_act + 28 * K_, [P, 3, TT, 8])
        ma = at("ma", o_act + 28 * K_ + 256, [P, TT, 4])
        brows = at("brows", o_act + 28 * K_ + 512, [4, 3, T])
        selh = at("selh", o_act + 31 * K_ + 512, [4, P])
        otok = at("otok", o_act, [P, TT, D])

        PS = ctx.enter_context(nc.psum_tensor("PS", [P, 8, 512], F32))

        def sem(name):
            return ctx.enter_context(nc.semaphore(name))

        raw_full = [sem(f"raw_full{s}") for s in range(4)]
        wh_ready = sem("wh_ready")
        wl_ready = sem("wl_ready")
        half_done = sem("half_done")
        psum_free = [sem("psum_free0"), sem("psum_free1")]
        act_ready = sem("act_ready")
        hid_ready = sem("hid_ready")
        mix_ready = sem("mix_ready")
        sq_done, hidh_done = sem("sq_done"), sem("hidh_done")
        start_full = [sem(f"start_full{s}") for s in range(4)]
        start_used = sem("start_used")
        mod_full = [sem("mod_full0"), sem("mod_full1")]
        mod_used = sem("mod_used")
        scaled = sem("scaled")
        acc_clear, fold_done, mod_ready = sem("acc_clear"), sem("fold_done"), sem("mod_ready")
        params_in, x_in, consts_ready = sem("params_in"), sem("x_in"), sem("consts_ready")
        c_in, c_mm, c_ready = sem("c_in"), sem("c_mm"), sem("c_ready")
        vecs_mm, vecs_ready = sem("vecs_mm"), sem("vecs_ready")
        xt_mm, xt_ready = sem("xt_mm"), sem("xt_ready")
        nsq_done, nstat_mm, nstd_done, xn_done, ah_done = (sem(n) for n in (
            "nsq_done", "nstat_mm", "nstd_done", "xn_done", "ah_done"))
        ot_mm, ot_ready, out_stored = sem("ot_mm"), sem("ot_ready"), sem("out_stored")
        g_names = ("wg_in", "gate_mm", "u", "nabs", "ln", "cum", "tmc", "ep", "en", "te", "keys", "sig",
                   "seg", "att_mm", "att", "masked", "o_mm", "o", "osq", "st_mm", "std", "res", "hh")
        g = {n: sem("g_" + n) for n in g_names}
        n_names = ("sq", "sq_mm", "ln", "std", "normed", "w1_in", "kdup_in", "kcp", "h_mm", "hexp", "hid", "kc_mm", "kcsq",
                   "kcsq_mm", "kcstd", "kcn", "kcd_clear", "kcd_in", "vc", "vsw_mm", "vsw", "gt_mm", "gexp", "cl_mm", "csub",
                   "cexp", "pc", "l_mm", "mx", "exp", "pn", "t_mm", "pt", "o_mm", "o", "hh")
        n_ = {n: sem("n_" + n) for n in n_names}
        m_names = ("tap", "cv", "sig", "silu", "gt_mm", "gcopy", "gabs", "gln", "lf", "b_mm", "rows", "a_mm",
                   "acol", "sel", "bc_mm", "dpre", "d", "em", "s_mm", "sd", "num_mm", "h", "hsq", "st_mm", "std", "hh",
                   "res")
        m_ = {n: sem("m_" + n) for n in m_names}
        dve_chain, act_chain = sem("dve_chain"), sem("act_chain")

        block = ctx.enter_context(nc.Block())
        done = [1 + (P_END + 1) // 2, 1 + P_END // 2]

        def banks(par):
            return PS[:, 2 * par:2 * par + 2, :].rearrange("p k (b t) -> p (k b) t", t=T)

        def raw_count(p, tail):
            return 16 * (p + 1 + (1 if tail else 0))

        def load_mod(eng, w, j, lo, width, slot, u):
            eng.wait_ge(mod_used, u + 1)
            eng.dma_start(modring[:, slot, 0:width], w[bass.ds(P * j, P), lo:lo + width]).then_inc(mod_full[slot], 16)

        def load_mod_row(eng, w, j, u):
            for k in range(4):
                load_mod(eng, w, j, 1536 * k, 1536, k % 2, u + k)

        def load_gate_row(eng, w, j, u):
            for k in range(2):
                load_mod(eng, w, j, 2 * D + 1024 * k, 1024, k, u + k)

        @block.sync
        def _(sp):
            def stage(src, col, p, s, cols=512):
                sp.wait_ge(wl_ready, 8 * p + 2 * s + 2)
                sp.dma_start(raw[:, s, :, 0:cols], rows_of(src, s, col, cols)).then_inc(raw_full[s], 16)

            def rows_of(src, s, col, cols):
                return src[512 * s:512 * s + 512, bass.ds(col, cols)].rearrange("(c p) n -> p c n", p=P)

            def store():
                for a in range(TT):
                    sp.wait_ge(ot_ready, 4 * a + 4)
                    sp.dma_start(out[0, P * a:P * a + P, :], otok[:, a, :]).then_inc(out_stored, 16)
                sp.wait_ge(out_stored, 16 * TT)

            sp.dma_start(xtok[:, :, :], x[0].rearrange("(a p) n -> p a n", p=P)).then_inc(x_in, 16)
            def start_piece(j, lo, width, k, n):
                sp.wait_ge(start_used, n + 1)
                sp.dma_start(startring[:, k, 0:width], mod_mix_w[0][bass.ds(P * j, P), lo:lo + width])\
                    .then_inc(start_full[k], 16)
            with sp.Fori(0, 4) as i:
                for k in range(4):
                    start_piece(4 * i + k, 0, D, k, 4 * i + k)
            with sp.Fori(0, 4) as i:
                for k in range(4):
                    start_piece(4 * i + k, D, D // 2, k, 16 + 4 * i + k)
            stage(ab_w_in[0], 0, 0, 0)
            with sp.Fori(0, 4) as i:
                for k in range(4):
                    start_piece(4 * i + k, D + D // 2, D // 2, k, 32 + 4 * i + k)

            w_in = ab_w_in[0]
            for s in range(1, 4):
                stage(w_in, 0, 0, s)
            for s in range(4):
                stage(w_in, 512, 1, s)
            with sp.Fori(1, 3) as i:
                for a in range(2):
                    for s in range(4):
                        stage(w_in, 512 * (2 * i + a), 2 * i + a, s)
            with sp.Fori(0, 2) as i:
                for a in range(2):
                    for s in range(4):
                        stage(w_in, GLA_COLS + 512 * (2 * i + a), 6 + 2 * i + a, s)
            for s in range(4):
                stage(w_in, GLA_COLS + 2048, 10, s)
            for s in range(4):
                sp.wait_ge(wl_ready, 8 * 11 + 2 * s + 2)
                for b, col in ((0, GLA_COLS - 16), (1, AB_COLS - P)):
                    sp.dma_start(raw[:, s, :, P * b:P * b + P], rows_of(w_in, s, col, P)).then_inc(raw_full[s], 16)
            for s in range(2):
                stage(ab_w_out[0], 0, P_OUT0, s)
            sp.wait_ge(act_ready, 4)
            sp.dma_start(wgate[:, :], gla_w_gate[0]).then_inc(g["wg_in"], 16)
            for s in range(2, 4):
                stage(ab_w_out[0], 0, P_OUT0, s)
            for a in range(1, 4):
                for s in range(4):
                    stage(ab_w_out[0], 512 * a, P_OUT0 + a, s)

            def mlp(l, p0):
                def quarter(q):
                    for a in range(8):
                        for s in range(4):
                            if a < 4:
                                stage(mlp_w1[l], D * q + 512 * a, p0 + 8 * q + a, s)
                            else:
                                sp.wait_ge(wl_ready, 8 * (p0 + 8 * q + a) + 2 * s + 2)
                                src = mlp_w2[l][bass.ds(D * q + 512 * s, 512), 512 * (a - 4):512 * (a - 3)]
                                sp.dma_start(raw[:, s, :, :], src.rearrange("(c p) n -> p c n", p=P))\
                                  .then_inc(raw_full[s], 16)
                with sp.Fori(0, 4) as q:
                    quarter(q)
            mlp(0, P_MLP0)
            with sp.Fori(0, 6) as i:
                for a in range(2):
                    for s in range(4):
                        stage(ml_w_in[0], 512 * (2 * i + a), P_PROJ1 + 2 * i + a, s)
            for s in range(4):
                stage(ml_w_in[0], ML_COLS - P, P_PROJ1 + 12, s, P)
            for s in range(2):
                stage(ml_w_out[0], 0, P_OUT1, s)
            for s in range(2, 4):
                stage(ml_w_out[0], 0, P_OUT1, s)
            for a in range(1, 4):
                for s in range(4):
                    stage(ml_w_out[0], 512 * a, P_OUT1 + a, s)
            mlp(1, P_MLP1)
            store()

        @block.scalar
        def _(act):
            chain = [0]

            def link(ins):
                chain[0] += 1
                ins.then_inc(act_chain, 1)
                act.wait_ge(act_chain, chain[0])

            fn = nc.scalar.activation

            def result():
                for s_, v in zip(psum_free, done):
                    act.wait_ge(s_, v)
                for k in range(8):
                    act.wait_ge(ot_mm, k + 1)
                    fn(otok[:, k // 4, 512 * (k % 4):512 * (k % 4) + 512], PS[:, k % 4, :], ACT.Copy).then_inc(ot_ready, 1)

            def weigh_piece(v, before):
                act.wait_ge(mod_full[v % 2], 16 * (before + v // 2) + 16)
                piece = modring[:, v % 2, :]
                fn(piece, piece, ACT.Identity, scale=siluc[:, v // 4:v // 4 + 1]).then_inc(scaled, 1)

            n_params = [0]

            def par(dst, src):
                n_params[0] += 1
                act.dma_start(dst, src).then_inc(params_in, 16)
            act.dma_start(prow[0:16, 0, :], c[0].rearrange("(m p) -> m p", p=P)).then_inc(c_in, 16)
            par(prow[16:48, 0, :], norm_mix_g.rearrange("l (m p) -> (l m) p", p=P))
            par(prow[48:80, 0, :], norm_mlp_g.rearrange("l (m p) -> (l m) p", p=P))
            par(prow[80:84, 0, :], gla_b_gate[0].rearrange("(m p) -> m p", p=P))
            par(prow[84:86, 0, :], gla_norm_g[0].rearrange("(m p) -> m p", p=P))
            for k in range(2):
                par(prow[86:87, 0, DH * k:DH * k + DH], nsa_q_norm_g)
                par(prow[87:88, 0, DH * k:DH * k + DH], nsa_k_norm_g)
                par(prow[92:124, 0, DH * k:DH * k + DH], nsa_cmp_pos_k[0])
                par(prow[64:96, 1, DH * k:DH * k + DH], nsa_cmp_pos_v[0])
                par((w2k, w2v)[0][DH * k:DH * k + DH, :], nsa_cmp_k_w2[0])
                par((w2k, w2v)[1][DH * k:DH * k + DH, :], nsa_cmp_v_w2[0])
            par(prow[88:92, 0, :], ml_norm_g[0].rearrange("(m p) -> m p", p=P))
            par(prow[0:64, 1, :], ml_conv_w[0].rearrange("j (m p) -> (j m) p", p=P))
            par(prow[0:96, 2, :], mod_mix_b.rearrange("l (m p) -> (l m) p", p=P))
            par(prow[0:96, 3, :], mod_mlp_b.rearrange("l (m p) -> (l m) p", p=P))
            par(brow[0:1, 0:4], ml_b_i)
            par(brow[0:1, 4:8], ml_b_f)
            assert n_params[0] == N_PARAMS

            act.wait_ge(c_mm, 1)
            fn(vecs[:, V_C:V_C + KC], PS[:, 5, 0:KC], ACT.Copy).then_inc(c_ready, 1)
            fn(siluc[:, :], PS[:, 5, 0:KC], ACT.Sigmoid).then_inc(c_ready, 1)
            act.wait_ge(vecs_mm, 1)
            fn(vecs[:, 16:124], PS[:, 4, 16:124], ACT.Copy)
            fn(vecs[:, 124:220], PS[:, 4, 128:224], ACT.Copy)
            fn(vecs[:, 220:316], PS[:, 4, 256:352], ACT.Copy)
            fn(vecs[:, 316:412], PS[:, 4, 384:480], ACT.Copy).then_inc(vecs_ready, 1)
            for k in range(8):
                act.wait_ge(xt_mm, k + 1)
                fn(xT[:, 2 * k:2 * k + 2, :].rearrange("p b t -> p (b t)"), PS[:, k % 4, :], ACT.Copy).then_inc(xt_ready, 1)

            def half(p, h, tail=False, cols=512):
                s = h // 2
                if h % 2 == 0:
                    act.wait_ge(raw_full[s], raw_count(p, tail))
                act.wait_ge(half_done, 8 * p + h + 1)
                fn(wh[:, h % 4, :, 0:cols], raw[:, s, 2 * (h % 2):2 * (h % 2) + 2, 0:cols], ACT.Copy)\
                    .then_inc(wh_ready, 1)

            def segment(p, before=None, first=4, tail=False, cols=512, tail2=None, cols2=512):
                tail2 = tail if tail2 is None else tail2
                for h in range(first, 8):
                    if before:
                        before(h)
                    half(p, h, tail, cols)
                for h in range(4):
                    half(p + 1, h, tail2, cols2)

            def panel_done(p):
                act.wait_ge(half_done, 8 * p + 12)

            def evac_proj(p, par, blk, nb=4, func=ACT.Copy):
                panel_done(p)
                fn(xproj[:, bass.ds(blk, nb), :], banks(par)[:, 0:nb, :], func).then_inc(psum_free[par], 1)

            def norm_squares(n, xready):
                for s_, v in xready:
                    act.wait_ge(s_, v)
                for k in range(4):
                    if k >= 2:
                        act.wait_ge(nstat_mm, 4 * n + k - 1)
                    fn(sqb[:, k % 2], xT[:, 4 * k:4 * k + 4, :], ACT.Square).then_inc(nsq_done, 1)

            def norm(n, xready=None, between=None):
                if xready:
                    norm_squares(n, xready)
                act.wait_ge(nstat_mm, 4 * n + 4)
                fn(std[:, :], PS[:, 5, 0:T], ACT.Sqrt, bias=eps[:, :], scale=1.0 / D).then_inc(nstd_done, 1)
                act.wait_ge(mod_ready, n + 1 + (n > 0))
                for k in range(4):
                    if n == 0 and k == 2:
                        between()
                        act.wait_ge(mod_ready, 2)
                    act.wait_ge(xn_done, 4 * n + k + 1)
                    for b in range(4):
                        m = 4 * k + b
                        ins = fn(xnb[:, k % 2, b, :], xnb[:, k % 2, b, :], ACT.Identity,
                                 scale=modv[:, 1, m:m + 1], bias=modv[:, 0, m:m + 1])
                    link(ins)
                    fn(act_hl[:, 4 * k:4 * k + 4, 0, :], xnb[:, k % 2], ACT.Copy).then_inc(ah_done, 1)

            norm_squares(0, [(xt_ready, 8)])
            act.wait_ge(consts_ready, N_CONSTS)
            norm(0, between=lambda: [half(0, h) for h in range(4)])
            for p in range(6):
                segment(p)
                if p in (2, 3):
                    panel_done(p)
                    fn(vt[:, :, 512 * (p - 2):512 * (p - 1)], PS[:, 2 * (p % 2):2 * (p % 2) + 2, :], ACT.Copy)\
                        .then_inc(psum_free[p % 2], 1)
                elif p in (4, 5):
                    panel_done(p)
                    fn(xproj[:, 4 * p:4 * p + 4, :], banks(p % 2), ACT.Sigmoid).then_inc(g["sig"], 1)
                else:
                    evac_proj(p, p % 2, 4 * p)
            with act.Fori(3, 5) as i:
                for a in range(2):
                    segment(2 * i + a)
                    evac_proj(2 * i + a, a, 8 * i + 4 * a)
            segment(10, tail=False, tail2=True, cols2=256)
            evac_proj(10, 0, 40)
            segment(11, tail=True, cols=256)
            panel_done(11)
            fn(xproj[:, GT, :], banks(1)[:, 1, :], ACT.Sigmoid)
            evac_proj(11, 1, ZT, 1)
            for h in range(GH):
                act.wait_ge(g["gate_mm"], 1)
                ins = fn(la[:, h, :], PS[:, 4 + h // 2, T * (h % 2):T * (h % 2) + T], ACT.Identity,
                         bias=vecs[:, V_BG + h:V_BG + h + 1])
            ins.then_inc(g["u"], 1)
            act.wait_ge(g["nabs"], 1)
            link(fn(ke[:, :, :], ke[:, :, :], ACT.Exp))
            fn(ke[:, :, :], ke[:, :, :], ACT.Ln, bias=ones[:, 0:1]).then_inc(g["ln"], 1)
            act.wait_ge(g["cum"], 1)
            fn(ep[:, :, :], cum[:, :, :], ACT.Exp, scale=1.0 / GTAU).then_inc(g["ep"], 1)
            fn(et[:, :, :], cum[:, :, GC - 1::GC], ACT.Exp, scale=1.0 / GTAU)
            fn(en[:, :, :], cum[:, :, :], ACT.Exp, scale=-1.0 / GTAU).then_inc(g["en"], 1)
            act.wait_ge(g["tmc"], 1)
            fn(seg[:, :, :], seg[:, :, :], ACT.Exp, scale=1.0 / GTAU).then_inc(g["te"], 1)
            for h in range(GH):
                act.wait_ge(g["att_mm"], h + 1)
                fn(att[:, h, :], PS[:, 4 + h, 0:384], ACT.Copy, scale=GDK ** -0.5).then_inc(g["att"], 1)
            def head_std(h):
                act.wait_ge(g["st_mm"], h + 1)
                fn(gstd[:, h, :], PS[:, 4 + h, 0:T], ACT.Sqrt, bias=eps[:, :], scale=1.0 / GDV).then_inc(g["std"], 1)
            for h in range(GH):
                act.wait_ge(g["o_mm"], h + 1)
                if h >= 2:
                    act.wait_ge(g["st_mm"], h - 1)
                fn(gsq[:, h % 2], PS[:, h, :].rearrange("p (v t) -> p v t", v=2), ACT.Square).then_inc(g["osq"], 1)
                fn(go[:, 2 * h:2 * h + 2, :], PS[:, h, :].rearrange("p (v t) -> p v t", v=2), ACT.Copy)\
                    .then_inc(g["o"], 1)
                if h >= 1:
                    head_std(h - 1)
            head_std(GH - 1)
            for k in range(2):
                act.wait_ge(g["res"], 2 * k + 2)
                fn(hid_hl[:, 4 * k:4 * k + 4, 0, :], xproj[:, GR + 4 * k:GR + 4 * k + 4, :], ACT.Copy)\
                    .then_inc(g["hh"], 1)
            fn(nt[:, 0:8, :], xproj[:, NQ:NQ + 8, :], ACT.Square)
            fn(nt[:, 8:10, :], xproj[:, SK:SK + 2, :], ACT.Square)
            fn(nt[:, 10:12, :], xproj[:, WK:WK + 2, :], ACT.Square).then_inc(n_["sq"], 1)
            act.wait_ge(n_["sq_mm"], 1)
            fn(nt[:, :, :], PS[:, 0:6, :].rearrange("p k (b t) -> p (k b) t", t=T), ACT.Ln, bias=eps[:, :],
               scale=1.0 / DH).then_inc(n_["ln"], 1)
            act.wait_ge(n_["ln"], 1)
            fn(nt[:, :, :], nt[:, :, :], ACT.Exp, scale=-0.5).then_inc(n_["std"], 1)
            act.wait_ge(n_["h_mm"], 1)
            fn(he[:, :, 0:30], PS[:, 4:6, 0:30], ACT.Sigmoid)
            fn(hk[:, :, 0:30], PS[:, 4:6, 0:30], ACT.Copy).then_inc(n_["hexp"], 1)
            act.wait_ge(n_["vsw_mm"], 1)
            act.wait_ge(n_["kcp"], 1)
            for k in range(2):
                fn(vsw[:, k], PS[:, 6 + k, :].rearrange("p (b d) -> p b d", b=2), ACT.Copy).then_inc(n_["vsw"], 1)
            act.wait_ge(n_["gt_mm"], 1)
            fn(gt[:, :, :], PS[:, 2, 0:256].rearrange("p (a f) -> p a f", a=2)[:, :, 80:128], ACT.Copy)\
                .then_inc(n_["gexp"], 1)
            act.wait_ge(n_["kc_mm"], 1)
            fn(kcs[:, 0:30], PS[:, 4, 64:94], ACT.Square).then_inc(n_["kcsq"], 1)
            fn(kcn[:, 0:30], PS[:, 4, 64:94], ACT.Copy)
            act.wait_ge(n_["kdup_in"], 128)
            fn(vcm[0:NCMP, :].rearrange("n (b g d) -> n g b d", b=2, g=2),
               PS[0:NCMP, 0:2, 0:P].rearrange("n g (b d) -> n g b d", b=2), ACT.Copy).then_inc(n_["vc"], 1)
            act.wait_ge(n_["kcsq_mm"], 1)
            fn(kcs[:, 0:30], PS[:, 5, 128:158], ACT.Sqrt, bias=eps[:, :], scale=1.0 / DH).then_inc(n_["kcstd"], 1)
            act.wait_ge(n_["csub"], 1)
            fn(sc[:, :, :, :], sc[:, :, :, :], ACT.Exp, scale=DH ** -0.5).then_inc(n_["cexp"], 1)
            def weights(h):
                b = h % 2
                act.wait_ge(n_["mx"], h + 1)
                for br in range(2):
                    for tt, (lo, hi) in enumerate(((0, P), (P, 384))):
                        ins = fn(pb[:, h % 3, br, lo:hi], pb[:, h % 3, br, lo:hi], ACT.Exp, scale=DH ** -0.5,
                                 bias=hst[:, b, 1, br, tt:tt + 1], accum_out=hst[:, b, 2, br, tt:tt + 1])
                ins.then_inc(n_["exp"], 1)
            weights(0)
            for h in range(NH):
                b = h % 2
                if h + 1 < NH:
                    weights(h + 1)
                act.wait_ge(n_["t_mm"], h + 1)
                if h >= 2:
                    act.wait_ge(n_["o_mm"], h - 1)
                fn(pt[:, b], PS[:, 4:6, 0:384], ACT.Copy)
                fn(ptc[0:NCMP, b, :].rearrange("n (a t) -> n a t", a=TT), PS[0:NCMP, 4:6, 384:512], ACT.Copy)\
                    .then_inc(n_["pt"], 1)
                if h % 2 == 0:
                    weigh_piece(40 + h // 2, 16)
            for k in range(2):
                act.wait_ge(n_["o"], 4 * k + 4)
                fn(hid_hl[:, 8 + 4 * k:12 + 4 * k, 0, :], nso[:, 4 * k:4 * k + 4, :], ACT.Copy).then_inc(n_["hh"], 1)

            for a in range(4):
                segment(P_OUT0 + a, tail=True)

            def mlp(l, p0, last):
                def quarter(q, final=False):
                    for a in range(8):
                        n = 16 * l + 4 * q + a

                        def before(h, a=a, n=n):
                            if 1 <= a <= 4 and h == 6:
                                act.wait_ge(sq_done, n)
                                fn(hid_hl[:, 4 * (a - 1):4 * a, 0, :], relu[:, :, :], ACT.Copy).then_inc(hidh_done, 1)
                        if final and a == 7:
                            for h in range(4, 8):
                                half(p0 + 8 * q + a, h, True)
                        else:
                            segment(p0 + 8 * q + a, before, tail=True)
                        if a < 4:
                            panel_done(p0 + 8 * q + a)
                            act.wait_ge(hid_ready, n + 1)
                            par = (p0 + a) % 2
                            fn(relu[:, :, :], banks(par), ACT.Relu).then_inc(psum_free[par], 1)
                with act.Fori(0, 3 if last else 4) as q:
                    quarter(q)
                if last:
                    quarter(3, True)

            norm(1, [(psum_free[0], P_MLP0 // 2 + 1), (psum_free[1], P_MLP0 // 2 + 1)])
            mlp(0, P_MLP0, False)
            norm(2, [(psum_free[0], P_PROJ1 // 2 + 1), (psum_free[1], P_PROJ1 // 2 + 1)])
            half(P_PROJ1, 4, True)
            with act.Fori(0, 2) as i:
                for a in range(2):
                    k = 2 * i + a
                    segment(P_PROJ1 + k, first=5, tail=True)
                    half(P_PROJ1 + k + 1, 4, True)
                    act.wait_ge(m_["cv"], k + 1)
                    act.wait_ge(m_["silu"], k + 1)
                    fn(xproj[:, 44:48, :], xproj[:, bass.ds(8 * i + 4 * a, 4), :], ACT.Sigmoid).then_inc(m_["sig"], 1)
            for k in range(4):
                p, a = P_PROJ1 + 4 + k, k % 2
                segment(p, first=5 if k == 0 else 4, tail=True)
                panel_done(p)
                fn(mvt[:, :, 512 * k:512 * k + 512], PS[:, 2 * a:2 * a + 2, :], ACT.Copy).then_inc(psum_free[a], 1)
            for k in range(4):
                segment(P_PROJ1 + 8 + k, tail=True, cols2=512 if k < 3 else P)
                if k == 3:
                    act.wait_ge(m_["silu"], 5)
                evac_proj(P_PROJ1 + 8 + k, k % 2, MO + 4 * k, func=ACT.Sigmoid)
            segment(P_PROJ1 + 12, tail=True, cols=P)
            panel_done(P_PROJ1 + 12)
            fn(gates[:, :], PS[:, 0, 0:T], ACT.Copy).then_inc(psum_free[0], 1)
            act.wait_ge(m_["gt_mm"], 1)
            fn(mg[:, 0], PS[:, 4, 0:256].rearrange("p (a f) -> p a f", a=2)[:, :, 120:128], ACT.Copy)\
                .then_inc(m_["gcopy"], 1)
            act.wait_ge(m_["gabs"], 1)
            link(fn(mg[:, 2, :, 4:8], mg[:, 1, :, 4:8], ACT.Exp))
            fn(mg[:, 2, :, 4:8], mg[:, 2, :, 4:8], ACT.Ln, bias=ones[:, 0:1]).then_inc(m_["gln"], 1)
            act.wait_ge(m_["a_mm"], 1)
            fn(ma[:, :, :], PS[:, 6, 0:16].rearrange("p (a f) -> p a f", a=2)[:, :, 0:4], ACT.Copy).then_inc(m_["acol"], 1)
            act.wait_ge(m_["acol"], 1)

            def decay(h):
                b = h % 2
                act.wait_ge(m_["dpre"], h + 1)
                fn(dm[:, b, 0:256], dm[:, b, 0:256], ACT.Exp, bias=ma[:, 0, h:h + 1])
                fn(dm[:, b, 256:384], dm[:, b, 256:384], ACT.Exp, bias=ma[:, 1, h:h + 1]).then_inc(m_["d"], 1)
                fn(mexp[:, :], PS[:, 5, T:2 * T], ACT.Exp, scale=-1.0).then_inc(m_["em"], 1)

            def round_heads(heads):
                for h in heads:
                    fn(hid_hl[:, 4 * h:4 * h + 4, 0, :], xproj[:, MO + 4 * h:MO + 4 * h + 4, :], ACT.Copy)\
                        .then_inc(m_["hh"], 1)
            decay(0)
            for h in range(MH):
                act.wait_ge(m_["h"], h + 1)
                fn(msq[:, :, :], mh[:, 4 * h:4 * h + 4, :], ACT.Square).then_inc(m_["hsq"], 1)
                if h + 1 < MH:
                    decay(h + 1)
                else:
                    act.wait_ge(m_["res"], 2)
                    act.wait_ge(m_["s_mm"], 4)
                    round_heads((0, 1))
                weigh_piece(36 + 3 * h, 80)
                act.wait_ge(m_["st_mm"], h + 1)
                if h >= 1:
                    act.wait_ge(m_["res"], h)
                fn(std[:, :], PS[:, 7, 0:T], ACT.Sqrt, bias=eps[:, :], scale=1.0 / MDV).then_inc(m_["std"], 1)
                weigh_piece(36 + 3 * h + 1, 80)
                weigh_piece(36 + 3 * h + 2, 80)
            act.wait_ge(m_["num_mm"], 4)
            for h in (2, 3):
                act.wait_ge(m_["res"], h + 1)
                round_heads((h,))
            for a in range(4):
                segment(P_OUT1 + a, tail=True)
            norm(3, [(psum_free[0], 34), (psum_free[1], 33)])
            mlp(1, P_MLP1, True)
            result()

        @block.gpsimd
        def _(pool):
            pool_n = [0]

            def step(ins):
                pool_n[0] += 1
                ins.then_inc(consts_ready, 1)
                pool.wait_ge(consts_ready, pool_n[0])
            ge = ALU.is_ge
            step(nc.gpsimd.memset(ident[:, :], 0.0))
            step(nc.gpsimd.affine_select(out=ident[:, :], in_=ident[:, :], compare_op=ALU.not_equal, fill=1.0,
                                         base=0, pattern=[[-1, P]], channel_multiplier=1))
            step(nc.gpsimd.memset(acc[:, :], 0.0))
            step(nc.gpsimd.memset(ones[:, :], 1.0))
            step(nc.gpsimd.memset(eps[:, :], EPS))
            step(nc.gpsimd.memset(pair_ones[:, :], 0.0))
            for k in range(2):
                step(nc.gpsimd.memset(pair_ones[DH * k:DH * k + DH, DH * k:DH * k + DH], 1.0))
            step(nc.gpsimd.memset(amask[:, :, :], 0.0))
            step(nc.gpsimd.affine_select(out=amask[:, 0::2, :], in_=amask[:, 0::2, :], compare_op=ge, fill=NEG,
                                         base=0, pattern=[[0, 2], [-1, P]], channel_multiplier=1))
            for k, (inside, outside) in enumerate(((0.0, NEG), (1.0, 0.0))):
                step(nc.gpsimd.memset(cmask[:, k], inside))
                step(nc.gpsimd.affine_select(out=cmask[:, k], in_=cmask[:, k], compare_op=ge, fill=outside,
                                             base=-31, pattern=[[P, TT], [-16, NCMP]], channel_multiplier=1))
            step(nc.gpsimd.memset(upper[:, :, :], 1.0))
            step(nc.gpsimd.affine_select(out=upper[:, 0, :], in_=upper[:, 0, :], compare_op=ge, fill=0.0,
                                         base=0, pattern=[[1, P]], channel_multiplier=-1))
            assert pool_n[0] == N_CONSTS
            with pool.Fori(0, 16) as i:
                load_gate_row(pool, mod_mix_w[0], i, 2 * i)
            pool.wait_ge(fold_done, 4)
            nc.gpsimd.memset(acc[:, :], 0.0).then_inc(acc_clear, 1)
            with pool.Fori(0, 5) as i:
                load_mod_row(pool, mod_mlp_w[0], i, 32 + 4 * i)
            pool.wait_ge(half_done, 4 + 8 * P_OUT0)
            nc.gpsimd.memset(seg[:, :, :], 1.0).then_inc(g["seg"], 1)
            pool.wait_ge(g["seg"], 1)
            nc.gpsimd.memset(seg[:, :, 0::GC], 0.0).then_inc(g["seg"], 1)

            def mlp0_row(j, pieces=range(4)):
                for k in pieces:
                    load_mod(pool, mod_mlp_w[0], j, 1536 * k, 1536, k % 2, 32 + 4 * j + k)
            mlp0_row(5)
            for h in range(GH):
                pool.wait_ge(g["att"], h + 1)
                v = att[:, h, :].rearrange("p (b t) -> p b t", t=P)[:, 0::2, :]
                nc.gpsimd.affine_select(out=v, in_=v, compare_op=ge, fill=0.0, base=0, pattern=[[0, 2], [1, P]],
                                        channel_multiplier=-1).then_inc(g["masked"], 1)
            for w, src, s_, v in ((w1k, nsa_cmp_k_w1, g["att_mm"], GH), (w1v, nsa_cmp_v_w1, g["res"], GH)):
                pool.wait_ge(s_, v)
                for k in range(2):
                    pool.dma_start(w[DH * k:DH * k + DH, :, :], src[0].rearrange("(l d) e -> d l e", d=DH))\
                        .then_inc(n_["w1_in"], 16)
                if w is w1k:
                    mlp0_row(6, range(2))
            mlp0_row(6, range(2, 4))
            mlp0_row(7, range(2))
            pool.wait_ge(n_["vsw_mm"], 1)
            nc.gpsimd.memset(kcd[:, :, :, :], 0.0).then_inc(n_["kcd_clear"], 1)
            pool.wait_ge(n_["normed"], 2)
            for br, blk in ((0, SK), (1, WK)):
                for gp in range(2):
                    for k in range(2):
                        pool.dma_start(kdup[DH * k:DH * k + DH, br, gp::2, :], xproj[DH * gp:DH * gp + DH, blk:blk + 2, :])\
                            .then_inc(n_["kdup_in"], 16)
            mlp0_row(7, range(2, 4))
            mlp0_row(8)
            mlp0_row(9, range(2))
            pool.wait_ge(n_["kcd_clear"], 1)
            pool.wait_ge(n_["kcn"], 1)
            for gp in range(2):
                for k in range(2):
                    pool.dma_start(kcd[DH * k:DH * k + DH, gp::2, k, :],
                                   kcn[DH * gp:DH * gp + DH, 0:30].rearrange("p (b n) -> p b n", b=2))\
                        .then_inc(n_["kcd_in"], 16)
            mlp0_row(9, range(2, 4))
            mlp0_row(10, range(2))
            for v in range(40, 48):
                pool.wait_ge(scaled, v - 39)
                pool.wait_ge(mod_used, 32 + v - 1)
                a = acc[:, 1536 * (v % 4):1536 * (v % 4) + 1536]
                nc.gpsimd.tensor_tensor(a, modring[:, v % 2, :], a, ALU.add).then_inc(mod_used, 1)
                mlp0_row((v + 2) // 4, [(v + 2) % 4])
            mlp0_row(12, range(2, 4))
            for j in range(13, 16):
                mlp0_row(j)
            pool.wait_ge(fold_done, 7)
            nc.gpsimd.memset(acc[:, :], 0.0).then_inc(acc_clear, 1)
            nc.gpsimd.memset(amask[:, :, :], 0.0).then_inc(acc_clear, 1)
            pool.wait_ge(acc_clear, 3)
            nc.gpsimd.affine_select(out=amask[:, 0::2, :], in_=amask[:, 0::2, :], compare_op=ge, fill=NEG,
                                    base=0, pattern=[[0, 2], [1, P]], channel_multiplier=-1).then_inc(acc_clear, 1)
            with pool.Fori(0, 16) as i:
                load_mod_row(pool, mod_mix_w[1], i, 96 + 4 * i)
            pool.wait_ge(fold_done, 10)
            nc.gpsimd.memset(acc[:, :], 0.0).then_inc(acc_clear, 1)
            with pool.Fori(0, 9) as i:
                load_mod_row(pool, mod_mlp_w[1], i, 160 + 4 * i)

            def mlp1_piece(v):
                load_mod(pool, mod_mlp_w[1], v // 4, 1536 * (v % 4), 1536, v % 2, 160 + v)
            mlp1_piece(36)
            mlp1_piece(37)
            for v in range(36, 48):
                pool.wait_ge(scaled, 8 + v - 35)
                pool.wait_ge(mod_used, 160 + v - 1)
                a = acc[:, 1536 * (v % 4):1536 * (v % 4) + 1536]
                nc.gpsimd.tensor_tensor(a, modring[:, v % 2, :], a, ALU.add).then_inc(mod_used, 1)
                mlp1_piece(v + 2)
            for v in range(50, 64):
                mlp1_piece(v)

        @block.vector
        def _(dve):
            V = nc.vector
            chain = [0]

            def link(ins):
                chain[0] += 1
                ins.then_inc(dve_chain, 1)
                dve.wait_ge(dve_chain, chain[0])

            dve.sem_inc(wl_ready, 8)
            dve.sem_inc(start_used, 4)
            dve.sem_inc(mod_used, 2)
            dve.sem_inc(hid_ready, 1)
            dve.sem_inc(m_["silu"], 1)
            dve.wait_ge(c_ready, 2)
            link(V.tensor_tensor(siluc[:, :], siluc[:, :], vecs[:, V_C:V_C + KC], ALU.mult))

            def accumulate(piece, j, lo, width):
                a = acc[:, lo:lo + width]
                return V.scalar_tensor_tensor(a, piece, siluc[:, bass.ds(j, 1)], a, ALU.mult, ALU.add)

            dve.wait_ge(consts_ready, 3)

            def start_piece(j, lo, width, k, full, n):
                dve.wait_ge(start_full[k], full)
                dve.wait_ge(start_used, n + 4)
                accumulate(startring[:, k, 0:width], j, lo, width).then_inc(start_used, 1)

            def start_chunk(lo, width, first, rows=(0, 4)):
                with dve.Fori(*rows) as i:
                    for k in range(4):
                        start_piece(4 * i + k, lo, width, k, 4 * first + 16 * i + 16, first + 4 * i + k)
            start_chunk(0, D, 0)
            start_chunk(D, D // 2, 16)

            def mod(j, lo, width, slot, uh, u, per_row):
                dve.wait_ge(mod_full[slot], 16 * uh + 16)
                dve.wait_ge(mod_used, u - per_row + 3)
                accumulate(modring[:, slot, 0:width], j, lo, width).then_inc(mod_used, 1)

            def mod_pieces(j, u):
                return [lambda k=k: mod(j, 1536 * k, 1536, k % 2, uh_of(u, k), uu(u, k), 4) for k in range(4)]

            def uu(u, k):
                return u[0] + k

            def uh_of(u, k):
                return u[1] + k // 2

            def gate_pieces(j, row):
                return [lambda k=k: mod(j, 2 * D + 1024 * k, 1024, k, row, 2 * row + k, 2) for k in range(2)]

            def half(p, h, cols=512):
                dve.wait_ge(wh_ready, 8 * p + h + 1)
                V.tensor_tensor(wl[:, h % 4, :, 0:cols], raw[:, h // 2, 2 * (h % 2):2 * (h % 2) + 2, 0:cols],
                                wh[:, h % 4, :, 0:cols].bitcast(F32), ALU.subtract).then_inc(wl_ready, 1)

            def segment(p, pieces=(), before=None, first=4, cols=512, cols2=512):
                pieces = list(pieces)
                for k in range(first - 4, 8):
                    h = (k + 4) % 8
                    if before:
                        before(k)
                    if k < 4:
                        half(p, h, cols)
                    else:
                        half(p + 1, h, cols2)
                    if pieces and k >= 2:
                        pieces.pop(0)()
                for piece in pieces:
                    piece()

            def fold(n, k, lo, hi, bias, gcol, panels_out=(), bank=6):
                for s_, v in zip(psum_free, panels_out):
                    dve.wait_ge(s_, v)
                dve.wait_ge(fold_done, k)
                dst = modv[:, :, :].rearrange("p s m -> p (s m)")[:, lo:hi]
                ins = V.tensor_tensor(dst, PS[:, bank, lo:hi], vecs[:, bias + lo:bias + hi], ALU.add)
                link(ins)
                if gcol is not None:
                    V.scalar_tensor_tensor(modv[:, 1, :], modv[:, 1, :], 1.0, vecs[:, gcol:gcol + KC], ALU.add, ALU.mult)\
                        .then_inc(mod_ready, 1)

            def xn(n, k):
                if k >= 2:
                    dve.wait_ge(act_ready, 4 * n + k - 1)
                V.tensor_tensor(xnb[:, k % 2], xT[:, 4 * k:4 * k + 4, :],
                                std[:, :].unsqueeze(1).broadcast_to([P, 4, T]), ALU.mult).then_inc(xn_done, 1)

            def al(n, k):
                dve.wait_ge(ah_done, 4 * n + k + 1)
                V.tensor_tensor(act_hl[:, 4 * k:4 * k + 4, 1, :], xnb[:, k % 2],
                                act_hl[:, 4 * k:4 * k + 4, 0, :].bitcast(F32), ALU.subtract).then_inc(act_ready, 1)

            def norm(n, bias, gcol, panels_out):
                dve.wait_ge(nstd_done, n + 1)
                link(V.reciprocal(std[:, :], std[:, :]))
                xn(n, 0)
                xn(n, 1)
                fold(n, 3 * n + 3, 0, 2 * KC, bias, gcol)
                for k in range(4):
                    al(n, k)
                    if k + 2 < 4:
                        xn(n, k + 2)
                fold(n, 3 * n + 4, 2 * KC, 3 * KC, bias, None, panels_out, 7)

            def evac_add(p, ph, par, col):
                dve.wait_ge(half_done, 8 * p + 12)
                dve.wait_ge(psum_free[par], ph - 2)
                for b in range(4):
                    xb = xT[:, 4 * col + b, :]
                    ins = V.scalar_tensor_tensor(xb, banks(par)[:, b, :], modv[:, 2, 4 * col + b:4 * col + b + 1], xb,
                                                 ALU.mult, ALU.add)
                ins.then_inc(psum_free[par], 1)

            dve.wait_ge(vecs_ready, 1)
            dve.wait_ge(xt_ready, 8)
            dve.wait_ge(nstd_done, 1)
            link(V.reciprocal(std[:, :], std[:, :]))
            xn(0, 0)
            xn(0, 1)
            start_chunk(D + D // 2, D // 2, 32, (0, 2))
            fold(0, 2, 0, 3 * KC // 2, V_BMIX, None)
            scale_cols = [(0, KC // 2), (KC // 2, KC)]

            def scale_gain(lo, hi):
                V.scalar_tensor_tensor(modv[:, 1, lo:hi], modv[:, 1, lo:hi], 1.0, vecs[:, V_NMIX + lo:V_NMIX + hi], ALU.add,
                                       ALU.mult).then_inc(mod_ready, 1)
            scale_gain(*scale_cols[0])
            start_chunk(D + D // 2, D // 2, 32, (2, 3))
            al(0, 0)
            al(0, 1)
            xn(0, 2)
            xn(0, 3)
            half(0, 0)
            half(0, 1)
            start_chunk(D + D // 2, D // 2, 32, (3, 4))
            half(0, 2)
            half(0, 3)
            fold(0, 3, 3 * KC // 2, 2 * KC, V_BMIX, None)
            scale_gain(*scale_cols[1])
            al(0, 2)
            al(0, 3)
            with dve.Fori(0, 2) as i:
                segment(2 * i, sum((gate_pieces(5 * i + j, 5 * i + j) for j in range(3)), []))
                segment(2 * i + 1, sum((gate_pieces(5 * i + j, 5 * i + j) for j in range(3, 5)), []))
            for p, rows in ((4, (10, 11, 12)), (5, (13, 14, 15))):
                segment(p, sum((gate_pieces(j, j) for j in rows), []))
                dve.wait_ge(g["sig"], p - 3)
                V.tensor_tensor(xproj[:, 4 * p:4 * p + 4, :], banks(p % 2), xproj[:, 4 * p:4 * p + 4, :], ALU.mult)\
                    .then_inc(psum_free[p % 2], 1)
            dve.wait_ge(acc_clear, 1)
            with dve.Fori(0, 2) as i:
                segment(6 + 2 * i, mod_pieces(2 * i, (32 + 8 * i, 16 + 4 * i)))
                segment(7 + 2 * i, mod_pieces(2 * i + 1, (36 + 8 * i, 18 + 4 * i)))
            fold(0, 4, 2 * KC, 3 * KC, V_BMIX, None)
            segment(10, mod_pieces(4, (48, 24)), cols2=256)
            segment(11, cols=256)

            def mods(j):
                for piece in mod_pieces(j, (32 + 4 * j, 16 + 2 * j)):
                    piece()
            dve.wait_ge(g["u"], 1)
            V.scalar_tensor_tensor(ke[:, :, :], la[:, :, :], -1.0, la[:, :, :], ALU.mult, ALU.min)\
                .then_inc(g["nabs"], 1)
            dve.wait_ge(g["ln"], 1)
            link(V.scalar_tensor_tensor(la[:, :, :], la[:, :, :], 0.0, ke[:, :, :], ALU.min, ALU.subtract))
            dve.wait_ge(g["seg"], 2)
            V.tensor_tensor_scan(cum[:, :, :].rearrange("p h t -> p (h t)"), seg[:, :, :].rearrange("p h t -> p (h t)"),
                                 la[:, :, :].rearrange("p h t -> p (h t)"), 0.0, ALU.mult, ALU.add).then_inc(g["cum"], 1)
            dve.wait_ge(g["cum"], 1)
            c4 = cum[:, :, :].rearrange("p h (c t) -> p (h c) t", t=GC)
            V.tensor_tensor(seg[:, :, :].rearrange("p h (c t) -> p (h c) t", t=GC),
                            c4[:, :, GC - 1:GC].broadcast_to([P, GH * NC_, GC]), c4, ALU.subtract).then_inc(g["tmc"], 1)
            dve.wait_ge(g["ep"], 1)
            V.tensor_tensor(xproj[:, GQ:GQ + 4, :], xproj[:, GQ:GQ + 4, :], ep[:, :, :], ALU.mult)
            dve.wait_ge(g["te"], 1)
            link(V.tensor_tensor(ke[:, :, :], xproj[:, GK:GK + 4, :], seg[:, :, :], ALU.mult))
            dve.wait_ge(g["en"], 1)
            link(V.tensor_tensor(xproj[:, GK:GK + 4, :], xproj[:, GK:GK + 4, :], en[:, :, :], ALU.mult))

            def chunks(t, a):
                return t.rearrange("p h (c t) -> p h c t", t=GC)[:, :, a::2, :]
            kd = xproj[:, GK:GK + 4, :]
            V.tensor_copy(chunks(m13[:, :, :], 0), chunks(ke[:, :, :], 0))
            V.tensor_copy(chunks(m13[:, :, :], 1), chunks(kd, 1))
            V.tensor_tensor(u2[:, :, 0:GC], ke[:, :, 0:GC], et[:, :, 1:2].broadcast_to([P, GH, GC]), ALU.mult)
            link(V.tensor_copy(u2[:, :, GC:P], ke[:, :, GC:P]))
            V.tensor_tensor(u4[:, :, :], u2[:, :, :], et[:, :, 2:3].broadcast_to([P, GH, P]), ALU.mult)\
                .then_inc(g["keys"], 1)
            mods(5)
            for h in range(GH):
                dve.wait_ge(g["std"], h + 1)
                link(V.reciprocal(gstd[:, h, :], gstd[:, h, :]))
                for v in range(2):
                    ov = go[:, 2 * h + v, :]
                    ins = V.scalar_tensor_tensor(ov, ov, vecs[:, V_GLAG + v:V_GLAG + v + 1], gstd[:, h, :], ALU.mult,
                                                 ALU.mult)
                link(ins)
                rb = xproj[:, GR + 2 * h:GR + 2 * h + 2, :]
                V.tensor_tensor(rb, rb, go[:, 2 * h:2 * h + 2, :], ALU.mult).then_inc(g["res"], 1)
            for k in range(2):
                dve.wait_ge(g["hh"], k + 1)
                V.tensor_tensor(hid_hl[:, 4 * k:4 * k + 4, 1, :], xproj[:, GR + 4 * k:GR + 4 * k + 4, :],
                                hid_hl[:, 4 * k:4 * k + 4, 0, :].bitcast(F32), ALU.subtract).then_inc(mix_ready, 1)
            mods(6)
            dve.wait_ge(n_["std"], 1)
            for lo, blk, n, vcol in ((0, NQ, 8, V_QG), (8, SK, 2, V_KG), (10, WK, 2, V_KG)):
                xb = xproj[:, blk:blk + n, :]
                ins = V.scalar_tensor_tensor(xb, xb, vecs[:, vcol:vcol + 1], nt[:, lo:lo + n, :], ALU.mult, ALU.mult)
                if lo:
                    ins.then_inc(n_["normed"], 1)
            dve.wait_ge(n_["normed"], 2)
            for dst, blk, vcol in ((kcpk, CK, V_POSK), (kcpv, CV, V_POSV)):
                for b in range(2):
                    for a in range(2):
                        src = xproj[:, blk + b, 16 * a:16 * a + 240].rearrange("p (n r) -> p r n", r=16)
                        pos = vecs[:, vcol + 16 * a:vcol + 16 * a + 16].unsqueeze(2).broadcast_to([P, 16, NCMP])
                        ins = V.tensor_tensor(dst[:, 16 * a:16 * a + 16, b, :], src, pos, ALU.add)
            ins.then_inc(n_["kcp"], 1)
            mods(7)
            mods(8)
            dve.wait_ge(n_["hexp"], 1)
            V.tensor_tensor(hk[:, :, 0:30], hk[:, :, 0:30], he[:, :, 0:30], ALU.mult).then_inc(n_["hid"], 1)
            dve.wait_ge(n_["kcstd"], 1)
            link(V.reciprocal(kcs[:, 0:30], kcs[:, 0:30]))
            V.scalar_tensor_tensor(kcn[:, 0:30], kcn[:, 0:30], vecs[:, V_KG:V_KG + 1], kcs[:, 0:30], ALU.mult, ALU.mult)\
                .then_inc(n_["kcn"], 1)
            mods(9)
            dve.wait_ge(n_["gexp"], 1)
            dve.wait_ge(n_["cl_mm"], 1)
            lc = PS[:, 2, 0:480].rearrange("p (a h n) -> p a h n", a=TT, n=NCMP)

            def over_heads(m):
                return m.unsqueeze(2).broadcast_to([P, TT, NH, NCMP])

            def over_blocks(m):
                return m.unsqueeze(3).broadcast_to([P, TT, NH, NCMP])
            for a in range(TT):
                ins = V.tensor_tensor(sc[:, a], lc[:, a], cmask[:, 0, a].unsqueeze(1).broadcast_to([P, NH, NCMP]), ALU.add)
            link(ins)
            link(V.tensor_reduce(cst[:, 0], sc[:, :, :, :], AX.X, ALU.max))
            V.tensor_tensor(sc[:, :, :, :], sc[:, :, :, :], over_blocks(cst[:, 0]), ALU.subtract).then_inc(n_["csub"], 1)
            dve.wait_ge(n_["cexp"], 1)
            link(V.tensor_reduce(cst[:, 1], sc[:, :, :, :], AX.X, ALU.add))
            link(V.reciprocal(cst[:, 1], cst[:, 1]))
            gview = gt[:, :, :].rearrange("p a (h b) -> p a h b", b=3)
            link(V.tensor_tensor(cst[:, 1], cst[:, 1], gview[:, :, :, 0], ALU.mult))
            for a in range(TT):
                ins = V.tensor_tensor(sc[:, a], sc[:, a], cmask[:, 1, a].unsqueeze(1).broadcast_to([P, NH, NCMP]), ALU.mult)
            link(ins)
            V.tensor_tensor(sc[:, :, :, :], sc[:, :, :, :], over_blocks(cst[:, 1]), ALU.mult).then_inc(n_["pc"], 1)
            def pair_out(k):
                dve.wait_ge(n_["o_mm"], 2 * k + 2)
                V.tensor_copy(nso[:, k, :], PS[:, 6 + k % 2, 0:T]).then_inc(n_["o"], 1)

            dve.wait_ge(n_["kdup_in"], 128)
            def maxima(h):
                b = h % 2
                dve.wait_ge(n_["l_mm"], h + 1)
                if h >= 3:
                    dve.wait_ge(n_["t_mm"], h - 2)
                lb = PS[:, 2 * b:2 * b + 2, 0:384]
                mk = amask[:, :, :].rearrange("p b t -> p (b t)").unsqueeze(1).broadcast_to([P, 2, 384])
                link(V.tensor_tensor(pb[:, h % 3], lb, mk, ALU.add))
                V.tensor_reduce(hst[:, b, 0, :, 0], pb[:, h % 3, :, 0:P], AX.X, ALU.max)
                link(V.tensor_reduce(hst[:, b, 0, :, 1], pb[:, h % 3, :, P:384], AX.X, ALU.max))
                V.tensor_scalar(hst[:, b, 1], hst[:, b, 0], -DH ** -0.5, None, ALU.mult).then_inc(n_["mx"], 1)
            maxima(0)
            for h in range(NH):
                b = h % 2
                if h + 1 < NH:
                    maxima(h + 1)
                dve.wait_ge(n_["exp"], h + 1)
                link(V.reciprocal(hst[:, b, 3], hst[:, b, 2]))
                link(V.tensor_tensor(hst[:, b, 3], hst[:, b, 3], gview[:, :, h, 1:3].rearrange("p a b -> p b a"), ALU.mult))
                for br in range(2):
                    for tt, (lo, hi) in enumerate(((0, P), (P, 384))):
                        ins = V.tensor_scalar(pb[:, h % 3, br, lo:hi], pb[:, h % 3, br, lo:hi], hst[:, b, 3, br, tt:tt + 1], None,
                                              ALU.mult)
                ins.then_inc(n_["pn"], 1)
                if h % 2 == 0 and h >= 2:
                    pair_out(h // 2 - 1)
            pair_out(NH // 2 - 1)
            for k in range(2):
                dve.wait_ge(n_["hh"], k + 1)
                V.tensor_tensor(hid_hl[:, 8 + 4 * k:12 + 4 * k, 1, :], nso[:, 4 * k:4 * k + 4, :],
                                hid_hl[:, 8 + 4 * k:12 + 4 * k, 0, :].bitcast(F32), ALU.subtract).then_inc(mix_ready, 1)

            dve.wait_ge(mod_full[1], 16 * (16 + 24) + 16)
            for a in range(4):
                segment(P_OUT0 + a, mod_pieces(12 + a, (32 + 4 * (12 + a), 16 + 2 * (12 + a))))
                p = P_OUT0 + a
                evac_add(p, p // 2, p % 2, a)

            def mlp(l, p0, last, mods_):
                def quarter(q, final=False):
                    for a in range(8):
                        n = 16 * l + 4 * q + a

                        def before(k, a=a, n=n):
                            if not 1 <= a <= 4:
                                return
                            if k == 1:
                                dve.wait_ge(psum_free[(p0 + a - 1) % 2], (p0 + a - 1) // 2 + 4 * q + 2)
                                V.tensor_tensor(relu[:, :, :], relu[:, :, :], relu[:, :, :], ALU.mult)\
                                    .then_inc(sq_done, 1)
                            if k == 4:
                                dve.wait_ge(hidh_done, n)
                                V.tensor_tensor(hid_hl[:, 4 * (a - 1):4 * a, 1, :], relu[:, :, :],
                                                hid_hl[:, 4 * (a - 1):4 * a, 0, :].bitcast(F32), ALU.subtract)\
                                    .then_inc(hid_ready, 1)
                        pieces = []
                        if mods_ and a % 2 == 0:
                            j = 4 * q + a // 2
                            pieces = mod_pieces(j, (96 + 4 * j, 48 + 2 * j))
                        p = p0 + 8 * q + a
                        if final and a == 7:
                            for h in range(4, 8):
                                half(p, h)
                        else:
                            segment(p, pieces, before)
                        if a >= 4:
                            evac_add(p, (p0 + a) // 2 + 4 * q, (p0 + a) % 2, a - 4)
                with dve.Fori(0, 3 if last else 4) as q:
                    quarter(q)
                if last:
                    quarter(3, True)

            norm(1, V_BMLP, V_NMLP, (9, 9))
            dve.wait_ge(acc_clear, 2)
            mlp(0, P_MLP0, False, True)
            norm(2, V_BMIX + 48, V_NMIX + 16, (25, 25))
            dve.wait_ge(acc_clear, 5)

            def mods1(j):
                return mod_pieces(j, (160 + 4 * j, 80 + 2 * j))
            def conv(i, a):
                k = 2 * i + a
                dve.wait_ge(half_done, 8 * (P_PROJ1 + k) + 12)
                for tap in range(3, -1, -1):
                    d = 3 - tap
                    if d:
                        dve.wait_ge(m_["tap"], 3 * k + d)
                    for b in range(4):
                        m = 8 * i + 4 * a + b
                        wcol = vecs[:, bass.ds(V_CONV + 16 * tap + m, 1)]
                        if d == 0:
                            ins = V.tensor_scalar(xproj[:, bass.ds(m, 1), :].squeeze(1), banks(a)[:, b, :], wcol, None, ALU.mult)
                        else:
                            to = xproj[:, bass.ds(m, 1), d:T].squeeze(1)
                            ins = V.scalar_tensor_tensor(to, banks(a)[:, b, 0:T - d], wcol, to, ALU.mult, ALU.add)
                    if tap:
                        ins.then_inc(m_["tap"], 1)
                ins.then_inc(m_["cv"], 1)
                dve.wait_ge(m_["cv"], k + 1)
                dve.sem_inc(psum_free[a], 1)
                half(P_PROJ1 + k + 1, 4)
                dve.wait_ge(m_["sig"], k + 1)
                qk = xproj[:, bass.ds(8 * i + 4 * a, 4), :]
                V.tensor_tensor(qk, qk, xproj[:, 44:48, :], ALU.mult).then_inc(m_["silu"], 1)
            half(P_PROJ1, 4)
            with dve.Fori(0, 2) as i:
                for a in range(2):
                    segment(P_PROJ1 + 2 * i + a, first=5)
                    conv(i, a)
            proj_mods = sum((mods1(j) for j in range(9)), [])
            for k in range(8):
                segment(P_PROJ1 + 4 + k, proj_mods[(9 * k + 1) // 2:(9 * k + 10) // 2], first=5 if k == 0 else 4,
                        cols2=512 if k < 7 else P)
            segment(P_PROJ1 + 12, cols=P)
            dve.wait_ge(m_["gcopy"], 1)
            V.scalar_tensor_tensor(mg[:, 1, :, 4:8], mg[:, 0, :, 4:8], -1.0, mg[:, 0, :, 4:8], ALU.mult, ALU.min)\
                .then_inc(m_["gabs"], 1)
            dve.wait_ge(m_["gln"], 1)
            V.scalar_tensor_tensor(mg[:, 0, :, 4:8], mg[:, 0, :, 4:8], 0.0, mg[:, 2, :, 4:8], ALU.min, ALU.subtract)\
                .then_inc(m_["lf"], 1)
            dve.wait_ge(acc_clear, 4)
            V.tensor_copy(selh[0:4, :], ident[0:4, 0:1].broadcast_to([4, P])).then_inc(m_["sel"], 1)
            dve.wait_ge(m_["b_mm"], 1)
            link(V.tensor_copy(brows[0:4, 0, :], PS[0:4, 5, 0:T]))
            link(V.tensor_tensor(brows[0:4, 1, :], PS[0:4, 5, T:2 * T], brows[0:4, 0, :], ALU.subtract))
            link(V.tensor_tensor_scan(brows[0:4, 2, :], brows[0:4, 1, :], brows[0:4, 1, :], 0.0, ALU.max, ALU.max))
            V.tensor_tensor(brows[0:4, 0, :], brows[0:4, 0, :], brows[0:4, 2, :], ALU.add).then_inc(m_["rows"], 1)
            mrow = amask[:, :, :].rearrange("p b t -> p (b t)")

            def scores(h):
                b = h % 2
                dve.wait_ge(m_["bc_mm"], h + 1)
                if h >= 2:
                    dve.wait_ge(m_["sd"], h - 1)
                V.scalar_tensor_tensor(dm[:, b, 0:256], PS[:, 5, 0:T], -1.0, mrow[:, 0:256], ALU.mult, ALU.add)
                V.scalar_tensor_tensor(dm[:, b, 256:384], PS[:, 5, P:T], -1.0, mrow[:, 256:384], ALU.mult, ALU.add)\
                    .then_inc(m_["dpre"], 1)
                if h + 1 < MH:
                    V.tensor_copy(selh[0:4, :], ident[0:4, h + 1:h + 2].broadcast_to([4, P])).then_inc(m_["sel"], 1)
                dve.wait_ge(m_["s_mm"], h + 1)
                dve.wait_ge(m_["d"], h + 1)
                V.scalar_tensor_tensor(sd[:, b, :], PS[:, 4, 0:384], MDK ** -0.5, dm[:, b, :], ALU.mult, ALU.mult)\
                    .then_inc(m_["sd"], 1)

            def split_head(h):
                dve.wait_ge(m_["hh"], h + 1)
                V.tensor_tensor(hid_hl[:, 4 * h:4 * h + 4, 1, :], xproj[:, MO + 4 * h:MO + 4 * h + 4, :],
                                hid_hl[:, 4 * h:4 * h + 4, 0, :].bitcast(F32), ALU.subtract).then_inc(mix_ready, 1)
            scores(0)
            for h in range(MH):
                b = h % 2
                dve.wait_ge(m_["em"], h + 1)
                dve.wait_ge(m_["num_mm"], h + 1)
                if h >= 1:
                    dve.wait_ge(m_["h"], h)
                link(V.scalar_tensor_tensor(mden[:, :], PS[:, 6, 0:T], -1.0, mexp[:, :], ALU.mult, ALU.max))
                link(V.tensor_tensor(mden[:, :], PS[:, 6, 0:T], mden[:, :], ALU.max))
                link(V.reciprocal(mden[:, :], mden[:, :]))
                hb = mh[:, 4 * h:4 * h + 4, :]
                V.tensor_tensor(hb, PS[:, 2 * b:2 * b + 2, :].rearrange("p k (b t) -> p (k b) t", t=T),
                                mden[:, :].unsqueeze(1).broadcast_to([P, 4, T]), ALU.mult).then_inc(m_["h"], 1)
                if h + 1 < MH:
                    scores(h + 1)
                else:
                    split_head(0)
                    split_head(1)
                dve.wait_ge(m_["std"], h + 1)
                link(V.reciprocal(std[:, :], std[:, :]))
                for v in range(4):
                    ins = V.scalar_tensor_tensor(hb[:, v, :], hb[:, v, :], vecs[:, V_MLG + v:V_MLG + v + 1], std[:, :],
                                                 ALU.mult, ALU.mult)
                link(ins)
                og = xproj[:, MO + 4 * h:MO + 4 * h + 4, :]
                V.tensor_tensor(og, hb, og, ALU.mult).then_inc(m_["res"], 1)
            split_head(2)
            split_head(3)
            dve.wait_ge(mod_full[1], 16 * (80 + 24) + 16)
            for a in range(4):
                segment(P_OUT1 + a, mods1(12 + a))
                p = P_OUT1 + a
                evac_add(p, p // 2, p % 2, a)
            norm(3, V_BMLP + 48, V_NMLP + 16, (34, 33))
            mlp(1, P_MLP1, True, False)

        @block.tensor
        def _(pe):
            mm = nc.tensor.matmul
            pe.sem_inc(half_done, 4)
            pe.sem_inc(psum_free[0], 1)
            pe.sem_inc(psum_free[1], 1)

            def panel(p, ph, par, src, ready=None, nb=4):
                pe.wait_ge(psum_free[par], ph + 1)
                for h in range(8):
                    if ready and h % 2 == 0:
                        ready(h // 2)
                    pe.wait_ge(wl_ready, 8 * p + h + 9)
                    for kk in range(2):
                        kc = 2 * h + kk
                        for b in range(nb):
                            o_ = PS[:, 2 * par + b // 2, T * (b % 2):T * (b % 2) + T]
                            w_h, w_l = wh[:, h % 4, kk, P * b:P * b + P], wl[:, h % 4, kk, P * b:P * b + P]
                            mm(o_, w_h, src[:, kc, 0, :], start=(kc == 0 and b % 2 == 0), stop=False,
                               skip_group_check=True)
                            mm(o_, w_h, src[:, kc, 1, :], start=False, stop=False, skip_group_check=True)
                            ins = mm(o_, w_l, src[:, kc, 0, :], start=False, stop=(kc == KC - 1),
                                     skip_group_check=True)
                    ins.then_inc(half_done, 1)

            def panel_tokens(p, ph, par, src, ready):
                pe.wait_ge(psum_free[par], ph + 1)
                for h in range(8):
                    if h % 2 == 0:
                        ready(h // 2)
                    pe.wait_ge(wl_ready, 8 * p + h + 9)
                    for kk in range(2):
                        kc = 2 * h + kk
                        w_h, w_l = wh[:, h % 4, kk, :], wl[:, h % 4, kk, :]
                        for a in range(TT):
                            o_ = PS[:, 2 * par + a, :]
                            x_h, x_l = src[:, kc, 0, P * a:P * a + P], src[:, kc, 1, P * a:P * a + P]
                            mm(o_, x_h, w_h, start=(kc == 0), stop=False, skip_group_check=True)
                            mm(o_, x_h, w_l, start=False, stop=False, skip_group_check=True)
                            ins = mm(o_, x_l, w_h, start=False, stop=(kc == KC - 1), skip_group_check=True)
                    ins.then_inc(half_done, 1)

            def fold(lo, hi, sem_, value, bank=6):
                pe.wait_ge(sem_, value)
                for m in range(lo, hi):
                    ins = mm(PS[:, bank, m:m + 1], acc[:, P * m:P * m + P], ones[:, 0:1], start=True, stop=True)
                ins.then_inc(fold_done, 1)

            def norm(n):
                for k in range(4):
                    pe.wait_ge(nsq_done, 4 * n + k + 1)
                    for b in range(4):
                        ins = mm(PS[:, 5, 0:T], ones[:, :], sqb[:, k % 2, b, :], start=(k + b == 0),
                                 stop=(k == 3 and b == 3))
                    ins.then_inc(nstat_mm, 1)

            def norm_and_fold(n, pieces):
                fold(0, KC, mod_used, 2 + pieces)
                norm(n)
                fold(KC, 2 * KC, mod_used, 2 + pieces)
                fold(2 * KC, 3 * KC, mod_used, 2 + pieces, 7)

            def act_in(n):
                return lambda s: pe.wait_ge(act_ready, 4 * n + s + 1)

            def result():
                pe.wait_ge(psum_free[0], done[0])
                pe.wait_ge(psum_free[1], done[1])
                for k in range(8):
                    a, m0 = k // 4, 4 * (k % 4)
                    if k >= 4:
                        pe.wait_ge(ot_ready, k - 3)
                    for b in range(4):
                        ins = nc.tensor.transpose(PS[:, k % 4, P * b:P * b + P], xT[:, m0 + b, P * a:P * a + P], ident[:, :])
                    ins.then_inc(ot_mm, 1)

            pe.wait_ge(consts_ready, 2)
            pe.wait_ge(c_in, 16)
            nc.tensor.transpose(PS[:, 5, 0:16], prow[0:16, 0, :], ident[0:16, 0:16]).then_inc(c_mm, 1)
            pe.wait_ge(consts_ready, N_CONSTS)
            pe.wait_ge(params_in, 16 * N_PARAMS)
            for k, n in enumerate((124, 96, 96, 96)):
                ins = nc.tensor.transpose(PS[:, 4, P * k:P * k + n], prow[0:n, k, :], ident[0:n, 0:n])
            ins.then_inc(vecs_mm, 1)
            pe.wait_ge(x_in, 16)
            for k in range(8):
                if k >= 4:
                    pe.wait_ge(xt_ready, k - 3)
                for b in range(2):
                    for a in range(2):
                        m = 2 * k + b
                        ins = nc.tensor.transpose(PS[:, k % 4, T * b + P * a:T * b + P * a + P],
                                                  xtok[:, a, P * m:P * m + P], ident[:, :])
                ins.then_inc(xt_mm, 1)
            pe.wait_ge(c_ready, 2)
            norm(0)
            fold(0, KC, start_used, 4 + 16)
            fold(KC, 3 * KC // 2, start_used, 4 + 32)

            def first_in(s):
                if s == 1:
                    fold(3 * KC // 2, 2 * KC, start_used, 4 + 48)
                pe.wait_ge(act_ready, s + 1)
            panel(0, 0, 0, act_hl, first_in)
            panel(1, 0, 1, act_hl, act_in(0))
            for a in range(2):
                panel_tokens(2 + a, 1, a, act_hl, act_in(0))
            for a in range(2):
                panel(4 + a, 2, a, act_hl, act_in(0))
            fold(2 * KC, 3 * KC, mod_used, 2 + 32)
            with pe.Fori(3, 5) as i:
                for a in range(2):
                    panel(2 * i + a, i, a, act_hl, act_in(0))
            panel(10, 5, 0, act_hl, act_in(0))
            panel(11, 5, 1, act_hl, act_in(0), 2)
            pe.wait_ge(psum_free[0], 7)
            pe.wait_ge(psum_free[1], 7)
            pe.wait_ge(g["wg_in"], 16)
            for h in range(GH):
                ins = mm(PS[:, 4 + h // 2, T * (h % 2):T * (h % 2) + T], wgate[0:16, GDK * h:GDK * h + GDK],
                         xproj[0:16, ZT, :], start=True, stop=True)
            ins.then_inc(g["gate_mm"], 1)
            pe.wait_ge(g["keys"], 1)
            for h in range(GH):
                q = xproj[:, GQ + h, :]
                kdh = xproj[:, GK + h, :]
                for lo, keys, t0 in ((0, kdh[:, 0:P], 0), (GC, m13[:, h, 0:P], 1), (2 * GC, u2[:, h, :], 2),
                                     (3 * GC, u4[:, h, :], 3), (4 * GC, kdh[:, P:T], 2), (5 * GC, m13[:, h, P:T], 3)):
                    ins = mm(PS[:, 4 + h, lo:lo + GC], keys, q[:, GC * t0:GC * t0 + GC], start=True, stop=True)
                ins.then_inc(g["att_mm"], 1)
            def squares_sum(h):
                pe.wait_ge(g["osq"], h + 1)
                for v in range(2):
                    ins = mm(PS[:, 4 + h, 0:T], ones[:, :], gsq[:, h % 2, v, :], start=(v == 0), stop=(v == 1))
                ins.then_inc(g["st_mm"], 1)
            for h in range(GH):
                pe.wait_ge(g["masked"], h + 1)
                for v in range(2):
                    col = GDV * h + P * v
                    mm(PS[:, h, T * v:T * v + T], vt[:, 0, col:col + P], att[:, h, 0:T], start=True, stop=False)
                    ins = mm(PS[:, h, T * v + P:T * v + T], vt[:, 1, col:col + P], att[:, h, T:384], start=False,
                             stop=True)
                ins.then_inc(g["o_mm"], 1)
                if h >= 1:
                    squares_sum(h - 1)
            squares_sum(GH - 1)
            pe.wait_ge(g["o"], 4)
            pe.wait_ge(g["std"], 4)
            pe.wait_ge(n_["sq"], 1)
            for k in range(12):
                ins = mm(PS[:, k // 2, T * (k % 2):T * (k % 2) + T], pair_ones[:, :], nt[:, k, :], start=True, stop=True)
            ins.then_inc(n_["sq_mm"], 1)
            for k in range(2):
                for b, blk in enumerate((SV, SV + 1, WV, WV + 1)):
                    ins = nc.tensor.transpose(PS[:, 6 + k, P * b:P * b + P], xproj[:, blk, P * k:P * k + P], ident[:, :])
            ins.then_inc(n_["vsw_mm"], 1)
            pe.wait_ge(n_["std"], 1)
            for k in range(2):
                ins = nc.tensor.transpose(PS[:, 2, P * k:P * k + P], xproj[:, GT, P * k:P * k + P], ident[:, :])
            ins.then_inc(n_["gt_mm"], 1)
            pe.wait_ge(n_["kcp"], 1)
            for kv, (w, src) in enumerate(((w1k, kcpk), (w1v, kcpv))):
                pe.wait_ge(n_["w1_in"], 64)
                for l in range(32):
                    for gp in range(2):
                        r = slice(DH * gp, DH * gp + DH)
                        ins = mm(PS[r, 4 + kv, 0:30], w[r, l, :], src[r, l, :, :], start=(l == 0), stop=(l == 31))
            ins.then_inc(n_["h_mm"], 1)
            pe.wait_ge(n_["hid"], 1)
            for gp in range(2):
                r = slice(DH * gp, DH * gp + DH)
                mm(PS[r, 4, 64:94], w2k[r, :], hk[r, 0, 0:30], start=True, stop=True)
            for gp in range(2):
                r = slice(DH * gp, DH * gp + DH)
                for b in range(2):
                    ins = mm(PS[0:NCMP, gp, DH * b:DH * b + DH], hk[r, 1, NCMP * b:NCMP * b + NCMP], w2v[r, :],
                             start=True, stop=True)
            ins.then_inc(n_["kc_mm"], 1)
            pe.wait_ge(n_["kcsq"], 1)
            mm(PS[:, 5, 128:158], pair_ones[:, :], kcs[:, 0:30], start=True, stop=True).then_inc(n_["kcsq_mm"], 1)
            pe.wait_ge(n_["kcd_in"], 64)
            pe.wait_ge(n_["normed"], 2)
            pe.wait_ge(n_["gexp"], 1)
            for a in range(TT):
                for j in range(NH // 2):
                    col = NCMP * (NH * a + 2 * j)
                    ins = mm(PS[:, 2, col:col + 2 * NCMP], xproj[:, NQ + j, P * a:P * a + P],
                             kcd[:, j // 2, :, :].rearrange("p k n -> p (k n)"), start=True, stop=True)
            ins.then_inc(n_["cl_mm"], 1)

            def logits(h):
                b = h % 2
                r = slice(DH * b, DH * b + DH)
                if h >= 2:
                    pe.wait_ge(n_["mx"], h - 1)
                for br in range(2):
                    mm(PS[:, 2 * b + br, 0:P], xproj[r, NQ + h // 2, 0:P], kdup[r, br, h // 4, 0:P], start=True,
                       stop=True)
                    ins = mm(PS[:, 2 * b + br, P:384], xproj[r, NQ + h // 2, P:T], kdup[r, br, h // 4, :], start=True,
                             stop=True)
                ins.then_inc(n_["l_mm"], 1)

            def turned(h):
                b = h % 2
                pe.wait_ge(n_["pn"], h + 1)
                if h >= 1:
                    pe.wait_ge(n_["pt"], h)
                for br in range(2):
                    for k in range(3):
                        nc.tensor.transpose(PS[:, 4 + br, P * k:P * k + P], pb[:, h % 3, br, P * k:P * k + P],
                                            ident[:, :])
                for a in range(TT):
                    ins = mm(PS[0:NCMP, 4 + a, 384:512], sc[:, a, h, :], ident[:, :], start=True, stop=True)
                ins.then_inc(n_["t_mm"], 1)

            def values(h):
                b = h % 2
                r = slice(DH * b, DH * b + DH)
                gcol = DH * (h // 4)
                pe.wait_ge(n_["pt"], h + 1)
                if b == 0 and h >= 4:
                    pe.wait_ge(n_["o"], h // 2 - 1)
                o_ = PS[r, 6 + (h // 2) % 2, 0:T]
                for br in range(2):
                    v0, v1 = vsw[:, 0, br, gcol:gcol + DH], vsw[:, 1, br, gcol:gcol + DH]
                    mm(o_, v0, pt[:, b, br, 0:T], start=(br == 0), stop=False, skip_group_check=True)
                    mm(o_[:, P:T], v1, pt[:, b, br, T:384], start=False, stop=False, skip_group_check=True)
                ins = mm(o_, vcm[0:NCMP, gcol:gcol + DH], ptc[0:NCMP, b, :], start=False, stop=True,
                         skip_group_check=True)
                ins.then_inc(n_["o_mm"], 1)

            pe.wait_ge(n_["vc"], 1)
            pe.wait_ge(n_["kdup_in"], 128)
            logits(0)
            pe.wait_ge(n_["csub"], 1)
            logits(1)
            logits(2)
            pe.wait_ge(n_["pc"], 1)
            pe.wait_ge(n_["vsw"], 2)
            for h in range(NH):
                turned(h)
                if h + 3 < NH:
                    logits(h + 3)
                values(h)

            def mix_in(l):
                return lambda s: pe.wait_ge(mix_ready, 4 * l + s + 1)
            with pe.Fori(0, 2) as i:
                for a in range(2):
                    panel(P_OUT0 + 2 * i + a, P_OUT0 // 2 + i, a, hid_hl, mix_in(0))

            def mlp(l, p0):
                with pe.Fori(0, 4) as q:
                    with pe.Fori(0, 2) as i:
                        for a in range(2):
                            par = (p0 + a) % 2
                            panel(p0 + 8 * q + 2 * i + a, (p0 + a) // 2 + 4 * q + i, par, act_hl, act_in(2 * l + 1))
                    with pe.Fori(0, 2) as i:
                        for a in range(2):
                            par = (p0 + a) % 2
                            panel(p0 + 4 + 8 * q + 2 * i + a, (p0 + 4 + a) // 2 + 4 * q + i, par, hid_hl,
                                  lambda s: pe.wait_ge(hid_ready, 16 * l + 4 * q + s + 2))
            norm_and_fold(1, 96)
            mlp(0, P_MLP0)
            norm_and_fold(2, 160)
            with pe.Fori(0, 2) as i:
                for a in range(2):
                    panel(P_PROJ1 + 2 * i + a, P_PROJ1 // 2 + i, a, act_hl, act_in(2))
            with pe.Fori(0, 2) as i:
                for a in range(2):
                    panel_tokens(P_PROJ1 + 4 + 2 * i + a, P_PROJ1 // 2 + 2 + i, a, act_hl, act_in(2))
            with pe.Fori(0, 2) as i:
                for a in range(2):
                    panel(P_PROJ1 + 8 + 2 * i + a, P_PROJ1 // 2 + 4 + i, a, act_hl, act_in(2))
            panel(P_PROJ1 + 12, P_PROJ1 // 2 + 6, 0, act_hl, act_in(2), 1)
            pe.wait_ge(psum_free[0], P_PROJ1 // 2 + 7 + 1)
            pe.wait_ge(psum_free[1], P_PROJ1 // 2 + 6 + 1)
            for a in range(TT):
                mm(PS[:, 4, P * a + 120:P * a + 128], gates[:, P * a:P * a + P], ident[:, 120:128], start=True,
                   stop=False, skip_group_check=True)
                ins = mm(PS[:, 4, P * a + 120:P * a + 128], ones[0:1, :], brow[0:1, :], start=False, stop=True,
                         skip_group_check=True)
            ins.then_inc(m_["gt_mm"], 1)
            pe.wait_ge(m_["lf"], 1)
            mm(PS[0:4, 5, 0:T], mg[:, 0, 0, 4:8], upper[:, :, :].rearrange("p a t -> p (a t)"), start=True, stop=False,
               skip_group_check=True)
            mm(PS[0:4, 5, P:T], mg[:, 0, 1, 4:8], upper[:, 0, :], start=False, stop=True, skip_group_check=True)
            for a in range(TT):
                ins = mm(PS[0:4, 5, T + P * a:T + P * a + P], mg[:, 0, a, 0:4], ident[:, :], start=True, stop=True)
            ins.then_inc(m_["b_mm"], 1)
            pe.wait_ge(m_["rows"], 1)
            for a in range(TT):
                ins = mm(PS[:, 6, 8 * a:8 * a + 4], brows[0:4, 1, P * a:P * a + P], ident[0:4, 0:4], start=True, stop=True)
            ins.then_inc(m_["a_mm"], 1)
            pe.wait_ge(m_["gcopy"], 1)
            pe.wait_ge(m_["acol"], 1)
            pe.wait_ge(m_["silu"], 5)

            def scores(h):
                if h >= 1:
                    pe.wait_ge(m_["dpre"], h)
                    pe.wait_ge(m_["em"], h)
                pe.wait_ge(m_["sel"], h + 1)
                mm(PS[:, 5, 0:T], selh[0:4, :], brows[0:4, 2, :], start=True, stop=True)
                mm(PS[:, 5, T:2 * T], selh[0:4, :], brows[0:4, 0, :], start=True, stop=True).then_inc(m_["bc_mm"], 1)
                if h >= 1:
                    pe.wait_ge(m_["sd"], h)
                for kc in range(2):
                    qh, kh = xproj[:, MQ + 2 * h + kc, :], xproj[:, MK + 2 * h + kc, :]
                    mm(PS[:, 4, 0:T], kh[:, 0:P], qh, start=(kc == 0), stop=False, skip_group_check=True)
                    ins = mm(PS[:, 4, T:384], kh[:, P:T], qh[:, P:T], start=False, stop=(kc == 1), skip_group_check=True)
                ins.then_inc(m_["s_mm"], 1)
            scores(0)
            for h in range(MH):
                b = h % 2
                pe.wait_ge(m_["sd"], h + 1)
                if h >= 1:
                    pe.wait_ge(m_["h"], h)
                mm(PS[:, 6, 0:T], ones[:, :], sd[:, b, 0:T], start=True, stop=False)
                mm(PS[:, 6, P:T], ones[:, :], sd[:, b, T:384], start=False, stop=True)
                for v in range(4):
                    col = MDV * h + P * v
                    bank, t0 = 2 * b + v // 2, T * (v % 2)
                    mm(PS[:, bank, t0:t0 + T], mvt[:, 0, col:col + P], sd[:, b, 0:T], start=True, stop=False)
                    ins = mm(PS[:, bank, t0 + P:t0 + T], mvt[:, 1, col:col + P], sd[:, b, T:384], start=False, stop=True)
                ins.then_inc(m_["num_mm"], 1)
                if h + 1 < MH:
                    scores(h + 1)
                pe.wait_ge(m_["hsq"], h + 1)
                for v in range(4):
                    ins = mm(PS[:, 7, 0:T], ones[:, :], msq[:, v, :], start=(v == 0), stop=(v == 3))
                ins.then_inc(m_["st_mm"], 1)
            for a in range(4):
                p = P_OUT1 + a
                panel(p, p // 2, p % 2, hid_hl, mix_in(1))
            norm_and_fold(3, 224)
            mlp(1, P_MLP1)
            result()


_INS = ['x', 'c', 'norm_mix_g', 'mod_mix_w', 'mod_mix_b', 'norm_mlp_g', 'mod_mlp_w', 'mod_mlp_b', 'mlp_w1', 'mlp_w2',
        'ab_w_in', 'ab_w_out', 'gla_w_gate', 'gla_b_gate', 'gla_norm_g', 'nsa_q_norm_g', 'nsa_k_norm_g',
        'nsa_cmp_pos_k', 'nsa_cmp_pos_v', 'nsa_cmp_k_w1', 'nsa_cmp_k_w2', 'nsa_cmp_v_w1', 'nsa_cmp_v_w2', 'ml_w_in',
        'ml_w_out', 'ml_conv_w', 'ml_b_i', 'ml_b_f', 'ml_norm_g']


def kernel(**inputs):
    import numpy as _np
    import concourse.bacc as _bacc
    from concourse import mybir as _mybir
    from concourse.bass_utils import run_bass_kernel_spmd as _run

    nc = _bacc.Bacc("TRN2", target_bir_lowering=False, num_devices=1)
    arrays, args = {}, []
    for name in _INS:
        a = _np.ascontiguousarray(inputs[name])
        arrays[f"in_{name}_dram"] = a
        args.append(nc.dram_tensor(f"in_{name}_dram", a.shape, _mybir.dt.from_np(a.dtype), kind="ExternalInput").ap())
    out = nc.dram_tensor("out_dram", (1, T, D), F32, kind="ExternalOutput").ap()
    trunk(nc, *args, out)
    r = _run(nc, [arrays], core_ids=[0])
    return r.results[0]["out_dram"]
```
